# Optimizing a Trainium2 kernel written in Bass

```python
import jax, jax.numpy as jnp
from jax import lax
import numpy as np

D_MODEL = 2048
BATCH = 1
SEQ = 256
DEPTH = 2

N_A = DEPTH // 2
N_B = DEPTH - N_A
RET_DIM = 256
RET_HEADS = D_MODEL // RET_DIM
RET_WIDTH = RET_HEADS * RET_DIM
RET_CHUNK = 128
RET_THETA = 10000.0
SWA_DIM = 64
SWA_HEADS = D_MODEL // SWA_DIM
SWA_KV_HEADS = SWA_HEADS // 8
SWA_WIDTH = SWA_HEADS * SWA_DIM
SWA_KV_WIDTH = SWA_KV_HEADS * SWA_DIM
WINDOW = 128
ROPE_THETA = 500000.0
ROT_DIM = SWA_DIM // 4
MEM_TOKENS = 256
MEM_HEADS = 4
MEM_DIM = D_MODEL // 8
MEM_WIDTH = MEM_HEADS * MEM_DIM
IN_A = 4 * RET_WIDTH + 2 * MEM_WIDTH
IN_B = 2 * SWA_WIDTH + 2 * MEM_WIDTH
MIX_WIDTH = RET_WIDTH + MEM_WIDTH
EPS = 1e-6

kernel_name = "yoco_retention_swa_sinks_memxattn"

def rms_norm(x, g):
    xf = x.astype(jnp.float32)
    y = xf * lax.rsqrt(jnp.mean(xf * xf, axis=-1, keepdims=True) + EPS)
    return (y * g.astype(jnp.float32)).astype(x.dtype)

def head_rms(x):
    xf = x.astype(jnp.float32)
    return xf * lax.rsqrt(jnp.mean(xf * xf, axis=-1, keepdims=True) + EPS)

def rope(x, positions, rot_dim, theta):
    inv = theta ** (-jnp.arange(0, rot_dim, 2, dtype=jnp.float32) / rot_dim)
    ang = positions.astype(jnp.float32)[..., None] * inv
    cos = jnp.cos(ang)[:, :, None, :].astype(x.dtype)
    sin = jnp.sin(ang)[:, :, None, :].astype(x.dtype)
    half = rot_dim // 2
    x1, x2, rest = x[..., :half], x[..., half:rot_dim], x[..., rot_dim:]
    return jnp.concatenate([x1 * cos - x2 * sin, x2 * cos + x1 * sin, rest], axis=-1)

def retention_chunkwise(q, k, v):
    B, S, H, dk = q.shape
    dv = v.shape[-1]
    C = RET_CHUNK
    N = S // C
    f32 = jnp.float32
    log_gamma = jnp.log(1.0 - jnp.exp2(-5.0 - jnp.arange(H, dtype=f32)))

    def to_chunks(t):
        return t.astype(f32).reshape(B, N, C, H, t.shape[-1]).transpose(1, 0, 3, 2, 4)

    qc, kc, vc = to_chunks(q), to_chunks(k), to_chunks(v)
    idx = jnp.arange(C, dtype=f32)
    diff = idx[:, None] - idx[None, :]
    decay = jnp.where(diff[None] >= 0,
                      jnp.exp(log_gamma[:, None, None] * jnp.maximum(diff, 0.0)[None]), 0.0)
    xi = jnp.exp(log_gamma[:, None] * (idx + 1.0))[:, :, None]
    zeta = jnp.exp(log_gamma[:, None] * (C - 1.0 - idx))[:, :, None]
    g_chunk = jnp.exp(log_gamma * C)[:, None, None]

    def step(R, inp):
        q_, k_, v_ = inp
        inner = jnp.einsum('bhnd,bhmd->bhnm', q_, k_) * decay
        o = (jnp.einsum('bhnm,bhmv->bhnv', inner, v_)
             + jnp.einsum('bhnd,bhdv->bhnv', q_ * xi, R))
        R = R * g_chunk + jnp.einsum('bhmd,bhmv->bhdv', k_ * zeta, v_)
        return R, o

    R0 = jnp.zeros((B, H, dk, dv), f32)
    _, o = lax.scan(step, R0, (qc, kc, vc))
    return o.transpose(1, 0, 3, 2, 4).reshape(B, S, H, dv)

def swa_sinks(q, k, v, sinks):
    B, S, Hq, d = q.shape
    Hkv = k.shape[2]
    G = Hq // Hkv
    W = WINDOW
    N = S // W
    qb = q.reshape(B, N, W, Hkv, G, d)
    kb = k.reshape(B, N, W, Hkv, d)
    vb = v.reshape(B, N, W, Hkv, d)
    zeros = jnp.zeros_like(kb[:, :1])
    kk = jnp.concatenate([jnp.concatenate([zeros, kb[:, :-1]], axis=1), kb], axis=2)
    vv = jnp.concatenate([jnp.concatenate([zeros, vb[:, :-1]], axis=1), vb], axis=2)
    s = jnp.einsum('bnqkgd,bnjkd->bnkgqj', qb, kk).astype(jnp.float32) * (d ** -0.5)
    qi = jnp.arange(W)[:, None] + W
    kj = jnp.arange(2 * W)[None, :]
    rel = qi - kj
    band = (rel >= 0) & (rel < W)
    not_pad = (jnp.arange(N)[:, None, None] > 0) | (kj[None] >= W)
    mask = band[None] & not_pad
    s = jnp.where(mask[None, :, None, None], s, -1e30)
    sink = sinks.astype(jnp.float32).reshape(1, 1, Hkv, G, 1, 1)
    m = jnp.maximum(jnp.max(s, axis=-1, keepdims=True), sink)
    p = jnp.exp(s - m)
    denom = jnp.sum(p, axis=-1, keepdims=True) + jnp.exp(sink - m)
    p = (p / denom).astype(v.dtype)
    o = jnp.einsum('bnkgqj,bnjkd->bnqkgd', p, vv)
    return o.reshape(B, S, Hq * d)

def mem_attention(qm, mk, mv):
    s = jnp.einsum('bshd,bmhd->bhsm', qm, mk).astype(jnp.float32) * (qm.shape[-1] ** -0.5)
    p = jax.nn.softmax(s, axis=-1).astype(mv.dtype)
    o = jnp.einsum('bhsm,bmhd->bshd', p, mv)
    return o.reshape(qm.shape[0], qm.shape[1], -1)

def setup_inputs(seed: int = 0) -> dict:
    key = jax.random.key(seed)
    ks = jax.random.split(key, 14)
    f32 = jnp.float32

    def w(k, shape, fan_in):
        return jax.random.normal(k, shape, f32) * (fan_in ** -0.5)

    x = jax.random.normal(ks[0], (BATCH, SEQ, D_MODEL), f32)
    mem = jax.random.normal(ks[1], (BATCH, MEM_TOKENS, D_MODEL), f32)
    positions = (jax.random.randint(ks[2], (BATCH, 1), 0, 1024, dtype=jnp.int32)
                 + jnp.arange(SEQ, dtype=jnp.int32)[None, :])
    pre_norm_g = 1.0 + 0.05 * jax.random.normal(ks[3], (DEPTH, D_MODEL), f32)
    post_norm_g = 1.0 + 0.05 * jax.random.normal(ks[4], (DEPTH, D_MODEL), f32)
    mem_norm_g = 1.0 + 0.05 * jax.random.normal(ks[5], (DEPTH, D_MODEL), f32)
    kv_norm_g = 1.0 + 0.05 * jax.random.normal(ks[6], (D_MODEL,), f32)
    w_in_a = w(ks[7], (N_A, D_MODEL, IN_A), D_MODEL)
    w_in_b = w(ks[8], (N_B, D_MODEL, IN_B), D_MODEL)
    w_kv_b = w(ks[9], (D_MODEL, 2 * SWA_KV_WIDTH), D_MODEL)
    sinks_b = 0.5 * jax.random.normal(ks[10], (N_B, SWA_HEADS), f32)
    w_mem_kv = w(ks[11], (DEPTH, D_MODEL, 2 * MEM_WIDTH), D_MODEL)
    w_out = w(ks[12], (DEPTH, MIX_WIDTH, D_MODEL), MIX_WIDTH)
    return {"x": x, "mem": mem, "positions": positions,
            "pre_norm_g": pre_norm_g, "post_norm_g": post_norm_g,
            "mem_norm_g": mem_norm_g, "kv_norm_g": kv_norm_g,
            "w_in_a": w_in_a, "w_in_b": w_in_b, "w_kv_b": w_kv_b,
            "sinks_b": sinks_b, "w_mem_kv": w_mem_kv, "w_out": w_out}

def reference(x, mem, positions, pre_norm_g, post_norm_g, mem_norm_g, kv_norm_g,
              w_in_a, w_in_b, w_kv_b, sinks_b, w_mem_kv, w_out):
    B, S, _ = x.shape
    M = mem.shape[1]
    h = x
    k_shared = None
    v_shared = None
    for l in range(DEPTH):
        y = rms_norm(h, pre_norm_g[l])
        mkv = rms_norm(mem, mem_norm_g[l]) @ w_mem_kv[l]
        mk = mkv[..., :MEM_WIDTH].reshape(B, M, MEM_HEADS, MEM_DIM)
        mv = mkv[..., MEM_WIDTH:].reshape(B, M, MEM_HEADS, MEM_DIM)
        if l < N_A:
            z = y @ w_in_a[l]
            q, k, v, g, qm, gm = jnp.split(
                z, np.cumsum([RET_WIDTH] * 4 + [MEM_WIDTH]).tolist(), axis=-1)
            q = rope(q.reshape(B, S, RET_HEADS, RET_DIM), positions, RET_DIM, RET_THETA)
            k = rope(k.reshape(B, S, RET_HEADS, RET_DIM), positions, RET_DIM, RET_THETA) * (RET_DIM ** -0.5)
            v = v.reshape(B, S, RET_HEADS, RET_DIM)
            o_main = head_rms(retention_chunkwise(q, k, v)).astype(x.dtype).reshape(B, S, RET_WIDTH)
        else:
            z = y @ w_in_b[l - N_A]
            q, g, qm, gm = jnp.split(
                z, np.cumsum([SWA_WIDTH, SWA_WIDTH, MEM_WIDTH]).tolist(), axis=-1)
            q = rope(q.reshape(B, S, SWA_HEADS, SWA_DIM), positions, ROT_DIM, ROPE_THETA)
            o_main = swa_sinks(q, k_shared, v_shared, sinks_b[l - N_A])
        o_main = o_main * jax.nn.silu(g)
        o_mem = mem_attention(qm.reshape(B, S, MEM_HEADS, MEM_DIM), mk, mv) * jax.nn.silu(gm)
        out = jnp.concatenate([o_main, o_mem], axis=-1) @ w_out[l]
        h = h + rms_norm(out, post_norm_g[l])
        if l == N_A - 1:
            kv = rms_norm(h, kv_norm_g) @ w_kv_b
            k_shared = rope(kv[..., :SWA_KV_WIDTH].reshape(B, S, SWA_KV_HEADS, SWA_DIM),
                            positions, ROT_DIM, ROPE_THETA)
            v_shared = kv[..., SWA_KV_WIDTH:].reshape(B, S, SWA_KV_HEADS, SWA_DIM)
    return h


_drawn_inputs = setup_inputs


def setup_inputs(seed=0):
    import zlib

    import numpy as np

    out = dict(_drawn_inputs(seed))
    spreads = {}
    factors = {'mem_norm_g': 3.185, 'sinks_b': 16.509, 'kv_norm_g': 7.663}
    for name, (base, spread) in spreads.items():
        noise = np.random.default_rng([zlib.crc32(name.encode()), seed]).standard_normal(out[name].shape)
        drawn = base * np.exp(spread * noise) if base else spread * noise
        out[name] = __import__('jax').numpy.asarray(drawn.astype(out[name].dtype))
    for name, factor in factors.items():
        out[name] = (out[name] * factor).astype(out[name].dtype)
    return out
```

```python
from contextlib import ExitStack

import concourse.bass as bass
from concourse import mybir

F32 = mybir.dt.float32
F32R = mybir.dt.float32r
I32 = mybir.dt.int32
ALU = mybir.AluOpType
ACT = mybir.ActivationFunctionType
AX = mybir.AxisListType

P = 128
S = 256
T = S // P
D = 2048
KT = D // P
N = 512
CK = 2
RING = 4
AHEAD = 3
RET_HEADS, RET_DIM = 8, 256
SWA_HEADS, SWA_DIM, KV_HEADS, WINDOW = 32, 64, 4, 128
MEM_WIDTH = 1024
MIX = D + MEM_WIDTH
EPS = 1e-6
HALF = RET_DIM // 2
ROT = SWA_DIM // 4
RH = ROT // 2
FREQS = HALF + RH
BLK = KT // CK
OBLK = MIX // P // CK
GROUPS = 6
NB_PER_KV = 4

SECTIONS = {}
_c = _b = 0
for _name, _blocks, _len in (("KV0", 4, BLK), ("MEM0", 4, BLK), ("RET", 16, BLK), ("OUT0", 4, OBLK),
                             ("KV1", 4, BLK), ("SHARED", 1, BLK), ("MEM1", 4, BLK), ("SWA", 8, BLK),
                             ("OUT1", 4, OBLK)):
    SECTIONS[_name] = (_c, _b)
    _c += _blocks * _len
    _b += _blocks
CHUNKS = _c

TWO_PI_1 = 6.28125
TWO_PI_2 = 0.0019350051879882812
PI = 3.141592653589793
TWO_PI_3 = 2 * PI - TWO_PI_1 - TWO_PI_2
PI_DOWN = 3.1415925
TWO_PI = 2 * PI
ROUND = 12582912.0


class Count:

    def __init__(self):
        self.n, self.it, self.per, self.start = 0, None, 0, 0

    def enter(self, it, per):
        self.it, self.per, self.start = it, per, self.n

    def leave(self, passes):
        assert self.n - self.start == self.per, (self.n - self.start, self.per)
        self.n, self.it = self.start + self.per * passes, None

    def up(self, k=1):
        self.n += k
        return self.value

    @property
    def value(self):
        return self.n if self.it is None else self.it * self.per + self.n


def trunk(nc, x, mem, positions, pre_g, post_g, mem_g, kv_g, w_in_a, w_in_b, w_kv, sinks, w_mem, w_out,
          c_ident, c_freq, c_decay, c_band, out):
    ctx = ExitStack()
    with ctx:
        def sb(name, shape, dt=F32):
            return ctx.enter_context(nc.sbuf_tensor(name, shape, dt))

        def sem(name):
            return ctx.enter_context(nc.semaphore(name))

        a_hi = sb("a_hi", [P, KT, S], F32R)
        a_lo = sb("a_lo", [P, KT, S], F32R)
        b_hi = sb("b_hi", [P, MIX // P, S], F32R)
        b_lo = sb("b_lo", [P, MIX // P, S], F32R)
        raw = sb("raw", [P, RING, CK, N])
        weight_hi = sb("weight_hi", [P, RING, CK, N], F32R)
        weight_lo = sb("weight_lo", [P, RING, CK, N], F32R)
        h = sb("h", [P, T, D])
        nat = sb("nat", [P, T, D])
        work = sb("work", [P, 5 * 1024])
        mem_kt = sb("mem_kt", [P, MEM_WIDTH // P, S])
        mem_v = sb("mem_v", [P, T, MEM_WIDTH])
        shared_kt = sb("shared_kt", [P, KV_HEADS, S])
        shared_v = sb("shared_v", [P, T, KV_HEADS * SWA_DIM])
        swa_cos = sb("swa_cos", [P, T, RH])[:, :, :]
        swa_sin = sb("swa_sin", [P, T, RH])[:, :, :]
        ident = sb("ident", [P, P])
        band = sb("band", [P, 3 * P])
        gains = sb("gains", [P, P])
        sink_cols = sb("sink_cols", [P, SWA_HEADS])
        neg_sinks = sb("neg_sinks", [P, SWA_HEADS])
        stats = sb("stats", [P, 128])
        minus_half = sb("minus_half", [P, 4])
        ret_eps = sb("ret_eps", [P, 4])

        ret_cos = shared_kt[:, 0, :].rearrange("p (t f) -> p t f", t=T)
        ret_sin = shared_kt[:, 1, :].rearrange("p (t f) -> p t f", t=T)
        block = work[:, 0:1024].rearrange("p (t n) -> p t n", t=T)
        q_t = work[:, 1024:2048].rearrange("p (k s) -> p k s", k=4)
        gated = [work[:, 2048 + 1024 * i:3072 + 1024 * i].rearrange("p (t n) -> p t n", t=T) for i in range(2)]
        gate = work[:, 4096:5120].rearrange("p (t n) -> p t n", t=T)
        rope_a, rope_b = gate[:, 0, :], gate[:, 1, :]
        x_nat = work[:, 0:4096].rearrange("p (t n) -> p t n", t=T)
        post_gain = work[:, 0:2048]
        mem_tile = work[:, 2048:4096]
        junk = work[:, 4096:5120]
        gain_rows = work[:, 4096:4096 + P]
        nat_f = nat[:, :, :].rearrange("p t n -> p (t n)")
        k_t = nat_f[:, 0:1024].rearrange("p (k s) -> p k s", k=4)
        v_nat = nat_f[:, 1024:2048].rearrange("p (t n) -> p t n", t=T)
        masked = nat_f[:, 2048:2816].rearrange("p (h n) -> p h n", h=2)
        decay = nat_f[:, 2816:3584].rearrange("p (h n) -> p h n", h=2)
        mem_p = nat_f[:, 0:1024].rearrange("p (t h m) -> p t h m", t=T, h=2)
        mem_pt = nat_f[:, 1024:2048].rearrange("p (h m s) -> p h m s", h=2, m=2)
        swa_p = nat_f[:, 0:1536].rearrange("p (r e n) -> p r e n", r=2, e=2)
        swa_pt = nat_f[:, 1536:3072].rearrange("p (r e n) -> p r e n", r=2, e=2)
        swa_kt = nat_f[:, 3072:3584].rearrange("p (g s) -> p g s", g=2)
        swa_v = nat_f[:, 3584:3840].rearrange("p (t n) -> p t n", t=T)
        freq = band[:, 0:FREQS]
        angle, turns, cos_arg, sin_arg, over = (
            mem_v[:, :, :].rearrange("p t n -> p (t n)")[:, T * FREQS * i:T * FREQS * (i + 1)]
            .rearrange("p (t f) -> p t f", t=T) for i in range(5))
        ss_mem, rs_mem = stats[:, 0:2], stats[:, 2:4]
        ss_x, rs_x = stats[:, 4:6], stats[:, 6:8]
        ss_ret, rs_ret = stats[:, 8:12], stats[:, 12:16]
        ss_out = stats[:, 16:24].rearrange("p (t b) -> p t b", t=T)
        ss_post, rs_post = stats[:, 24:26], stats[:, 26:28]
        ss_h, rs_h = stats[:, 28:30], stats[:, 30:32]
        top, neg, den, inv = (stats[:, 32 + 4 * i:36 + 4 * i].rearrange("p (a b) -> p a b", a=2) for i in range(4))
        swa_top, swa_neg, swa_den, swa_es, swa_inv = (
            [stats[:, 48 + 8 * i + 4 * r:52 + 8 * i + 4 * r].rearrange("p (e b) -> p e b", e=2) for r in range(2)]
            for i in range(5))
        mean = stats[:, 88:92]
        pos_f = stats[:, 92:94]
        pos_i = sb("pos_i", [P, T], I32)

        acc = ctx.enter_context(nc.psum_tensor("acc", [P, 2, T, N], F32))
        aux = ctx.enter_context(nc.psum_tensor("aux", [P, 4, N], F32))
        turn = [aux[:, i, :] for i in range(2)]
        score = [aux[:, 2 + i, :] for i in range(2)]

        raw_in = [sem(f"raw_in{i}") for i in range(RING)]
        hi_ready, lo_ready = sem("hi_ready"), sem("lo_ready")
        chunk_done = sem("chunk_done")
        acc_drained = [sem("acc_drained0"), sem("acc_drained1")]
        ident_in, freq_in, band_in, gains_in, pos_in, sinks_in = (
            sem(n) for n in ("ident_in", "freq_in", "band_in", "gains_in", "pos_in", "sinks_in"))
        mem_in, x_in = sem("mem_in"), sem("x_in")
        post_in, mem_tile_in, decay_in = sem("post_in"), sem("mem_tile_in"), sem("decay_in")
        gains_turned, gains_ready = sem("gains_turned"), sem("gains_ready")
        freq_read, angles_ready, tables_ready = sem("freq_read"), sem("angles_ready"), sem("tables_ready")
        squares = sem("squares")
        half_ready, means, rsqrt_ready = sem("half_ready"), sem("means"), sem("rsqrt_ready")
        normed = sem("normed")
        norm_turned, norm_hi, norm_lo = sem("norm_turned"), sem("norm_hi"), sem("norm_lo")
        tile_normed = sem("tile_normed")
        tile_turned, tile_hi, tile_lo = sem("tile_turned"), sem("tile_hi"), sem("tile_lo")
        roped = sem("roped")
        block_turned = sem("block_turned")
        block_a, block_b = sem("block_a"), sem("block_b")
        score_full, o_full, o_stored = sem("score_full"), sem("o_full"), sem("o_stored")
        neg_ready, probs_ready, probs_turned = sem("neg_ready"), sem("probs_ready"), sem("probs_turned")
        probs_a, probs_b = sem("probs_a"), sem("probs_b")
        masked_ready = sem("masked_ready")
        tanh_ready, gated_ready, gated_turned = sem("tanh_ready"), sem("gated_ready"), sem("gated_turned")
        mix_hi, mix_lo = sem("mix_hi"), sem("mix_lo")
        out_squares, post_sum = sem("out_squares"), sem("post_sum")
        copies_ready = sem("copies_ready")
        h_ready, final_ready, out_done = sem("h_ready"), sem("final_ready"), sem("out_done")
        dve_step = sem("dve_step")

        R_MEM, R_X, R_RET, R_POST0, R_H, R_POST1 = 1, 2, 3, 7, 8, 9
        B_KV, B_MEM, B_RET, B_SHARED, B_SWA = (0, 12), (2, 15), 4, 14, 17
        ROPE_RET, ROPE_SHARED, ROPE_SWA = 0, 8, 9
        U_MEM, U_RET, U_SWA = (0, 6), 2, 8
        X_MEM, X_SWA = (0, 2), 4
        UNITS = 4

        def drained(eng, b, it=0, per=0):
            eng.wait_ge(acc_drained[b % 2], it * (per // 2) + (b // 2 + 1))

        def unit_slot(p, u):
            return 11 + BLK * p + 2 * u

        def units_at(s, after):
            return [(p, u) for p in range(2) for u in range(UNITS) if unit_slot(p, u) + after == s]

        def rows(w):
            return w.rearrange("(k p) n -> p k n", p=P)

        blk = ctx.enter_context(nc.Block())

        @blk.sync
        def _(sp):
            def load(c, slot, w, k, col):
                if not (isinstance(c, int) and c < RING):
                    sp.wait_ge(lo_ready, c - RING + 1)
                sp.dma_start(raw[:, slot], rows(w)[:, k:k + CK, bass.ds(col, N)]).then_inc(raw_in[slot], 16)

            def load_block(c, w, col):
                for i in range(BLK):
                    load(c + i, i % RING, w, CK * i, col)

            def kv(layer, first=0):
                c0 = SECTIONS[f"KV{layer}"][0]
                for b in range(4):
                    for i in range(BLK):
                        if b * BLK + i >= first:
                            load(c0 + b * BLK + i, i % RING, w_mem[layer], CK * i, N * b)

            def memory_blocks(layer, w, col):
                c0 = SECTIONS[f"MEM{layer}"][0]
                for b in range(4):
                    load_block(c0 + BLK * b, w, col + N * b)

            def out_blocks(layer):
                c0 = SECTIONS[f"OUT{layer}"][0]
                with sp.Fori(1, 3) as it:
                    for b in range(2):
                        for i in range(OBLK):
                            g = i // 2
                            k = (KT + 4 * g if g < 2 else 4 * (g - 2)) + CK * (i % 2)
                            load(it * (2 * OBLK) + (c0 + OBLK * (b - 2) + i), i % RING, w_out[layer], k,
                                 it * (2 * N) + N * (b - 2))

            for t in range(T):
                sp.dma_start(nat[:, t, :], mem[0, t * P:(t + 1) * P, :]).then_inc(mem_in, 16)
            for i in range(RING):
                load(i, i, w_mem[0], CK * i, 0)
            for t in range(T):
                sp.dma_start(h[:, t, :], x[0, t * P:(t + 1) * P, :]).then_inc(x_in, 16)
            kv(0, first=RING)
            memory_blocks(0, w_in_a[0], 4 * D)
            c0 = SECTIONS["RET"][0]
            with sp.Fori(0, 4) as it:
                for b in range(4):
                    load_block(it * (4 * BLK) + (c0 + BLK * b), w_in_a[0], it * N + D * b)
            out_blocks(0)
            kv(1)
            load_block(SECTIONS["SHARED"][0], w_kv, 0)
            memory_blocks(1, w_in_b[0], 2 * D)
            c0 = SECTIONS["SWA"][0]
            with sp.Fori(0, 2) as it:
                for b in range(4):
                    load_block(it * (4 * BLK) + (c0 + BLK * b), w_in_b[0],
                               it * (2 * N) + (D * (b // 2) + N * (b % 2)))
            out_blocks(1)
            for t in range(T):
                sp.wait_ge(final_ready, t + 1)
                sp.dma_start(out[0, t * P:(t + 1) * P, :], nat[:, t, :]).then_inc(out_done, 16)
            sp.wait_ge(out_done, 16 * T)

        @blk.gpsimd
        def _(pool):
            for r0, g in ((0, pre_g), (2 * KT, mem_g), (4 * KT, post_g)):
                pool.dma_start(gain_rows[r0:r0 + 2 * KT, :],
                               g.rearrange("l (k p) -> (l k) p", p=P)).then_inc(gains_in, 16)
            for r0 in (6 * KT, 7 * KT):
                pool.dma_start(gain_rows[r0:r0 + KT, :], kv_g.rearrange("(k p) -> k p", p=P)).then_inc(gains_in, 16)
            pool.dma_start(ident[:, :], c_ident).then_inc(ident_in, 16)
            pool.dma_start(pos_i[:, :], positions[0].rearrange("(t p) -> p t", p=P),
                           allow_slow_non_contiguous=True).then_inc(pos_in, 16)
            pool.dma_start(freq, c_freq).then_inc(freq_in, 16)
            pool.dma_start(sink_cols[:, :], sinks[0].partition_broadcast(P)).then_inc(sinks_in, 16)
            pool.memset(minus_half[:, :], -0.5)
            pool.memset(ret_eps[:, :], RET_DIM * EPS).then_inc(half_ready, 1)
            pool.wait_ge(half_ready, 1)

            n_means = Count()

            def rsqrt(total, result, scale, eps):
                width = total.shape[1]
                if not isinstance(n_means.value, int) or n_means.value:
                    pool.wait_ge(rsqrt_ready, n_means.value)
                pool.tensor_scalar(mean[:, 0:width], total, scale, eps, ALU.mult, ALU.add).then_inc(means, 1)
                pool.wait_ge(means, n_means.up())
                pool.tensor_tensor(result, mean[:, 0:width], minus_half[:, 0:width], ALU.pow).then_inc(rsqrt_ready, 1)

            pool.wait_ge(squares, 2)
            rsqrt(ss_mem, rs_mem, 1.0 / D, EPS)
            pool.wait_ge(squares, 4)
            rsqrt(ss_x, rs_x, 1.0 / D, EPS)
            pool.wait_ge(freq_read, 1)
            pool.dma_start(band[:, :], c_band).then_inc(band_in, 16)
            pool.wait_ge(norm_turned, KT // 2)
            with pool.Fori(0, 4) as it:
                n_means.enter(it, 1)
                pool.dma_start(decay, c_decay[:, bass.ds(it * 2, 2), :]).then_inc(decay_in, 16)
                pool.wait_ge(squares, it * 4 + 8)
                pool.tensor_tensor(mean, ss_ret, ret_eps[:, :], ALU.add).then_inc(means, 1)
                pool.wait_ge(means, n_means.up())
                pool.tensor_tensor(rs_ret, mean, minus_half[:, :], ALU.pow).then_inc(rsqrt_ready, 1)
            n_means.leave(4)
            pool.wait_ge(gated_turned, GROUPS)
            pool.dma_start(post_gain, post_g[0].partition_broadcast(P)).then_inc(post_in, 16)
            for t in range(T):
                if t:
                    pool.wait_ge(tile_turned, 4 * t)
                pool.dma_start(mem_tile, mem[0, t * P:(t + 1) * P, :]).then_inc(mem_tile_in, 16)
            pool.wait_ge(post_sum, 1)
            rsqrt(ss_post, rs_post, 1.0 / D, EPS)
            pool.wait_ge(squares, 22)
            rsqrt(ss_h, rs_h, 1.0 / D, EPS)
            pool.wait_ge(block_a, B_SHARED + 1)
            pool.wait_ge(block_b, B_SHARED + 1)
            with pool.Fori(0, 2) as it:
                pool.wait_ge(o_full, it * (2 * UNITS) + U_SWA)
                pool.tensor_copy(swa_kt, shared_kt[:, bass.ds(it * 2, 2), :])
                pool.tensor_copy(swa_v, shared_v[:, :, bass.ds(it * (2 * SWA_DIM), 2 * SWA_DIM)]).then_inc(copies_ready, 1)
            pool.wait_ge(gated_turned, 2 * GROUPS)
            pool.dma_start(post_gain, post_g[1].partition_broadcast(P)).then_inc(post_in, 16)
            pool.wait_ge(post_sum, 2)
            rsqrt(ss_post, rs_post, 1.0 / D, EPS)

        @blk.scalar
        def _(act):
            def copy(dst, src, **kw):
                return nc.scalar.activation(dst, src, ACT.Copy, **kw)

            def split(c, slot):
                if isinstance(c, int) and c >= CHUNKS:
                    return
                act.wait_ge(raw_in[slot], c * (16 // RING) + (16 - slot * (16 // RING)))
                if not (isinstance(c, int) and c < RING):
                    act.wait_ge(chunk_done, c - RING + 1)
                copy(weight_hi[:, slot], raw[:, slot]).then_inc(hi_ready, 1)

            def sum_squares(src, total, scratch):
                return nc.scalar.activation(scratch, src, ACT.Square, accum_out=total)

            def norm_part(g, dst, gain):
                act.wait_ge(norm_turned, g + 1)
                i = g % (KT // 2)
                for j in range(2):
                    last = copy(dst[:, 2 * i + j, :], aux[:, g % 4, S * j:S * (j + 1)],
                                scale=gains[:, gain + 2 * i + j:gain + 2 * i + j + 1])
                last.then_inc(norm_hi, 1)

            def copy_block(c_end, par, it=0):
                act.wait_ge(chunk_done, c_end)
                for t in range(T):
                    last = copy(block[:, t, :], acc[:, par, t, :])
                last.then_inc(acc_drained[par], 1)

            def store_half(n, dst):
                act.wait_ge(block_turned, n + 1)
                copy(dst, turn[0]).then_inc(block_a, 1)

            def mix_part(g, pos):
                act.wait_ge(gated_turned, g + 1)
                for i in range(2):
                    copy(b_hi[:, bass.ds(pos * 4 + 2 * i, 2), :], turn[i]).then_inc(mix_hi, 1)

            def tanh_gate(g, c_end, par):
                act.wait_ge(chunk_done, c_end)
                if not (isinstance(g, int) and g == 0):
                    act.wait_ge(gated_ready, g)
                for t in range(T):
                    nc.scalar.activation(gate[:, t, :], acc[:, par, t, :], ACT.Tanh, scale=0.5).then_inc(tanh_ready, 1)

            scratch = acc[:, :, :, :].rearrange("p a t n -> p (a t n)")
            for i, (src, total) in enumerate(((nat, ss_mem), (h, ss_x))):
                act.wait_ge((mem_in, x_in)[i], 16 * T)
                for t in range(T):
                    if i or t:
                        act.wait_ge(squares, T * i + t)
                    sum_squares(src[:, t, :], total[:, t:t + 1], scratch).then_inc(squares, 1)
            act.wait_ge(angles_ready, 2)
            for arg, ret, swa in ((cos_arg, ret_cos, swa_cos), (sin_arg, ret_sin, swa_sin)):
                nc.scalar.activation(ret, arg[:, :, 0:HALF], ACT.Sin)
                last = nc.scalar.activation(swa, arg[:, :, HALF:FREQS], ACT.Sin)
            last.then_inc(tables_ready, 1)
            for c in range(AHEAD):
                split(c, c)
            act.wait_ge(gains_ready, 1)
            for g in range(KT // 2):
                norm_part(g, b_hi, 2 * KT)

            def kv(layer):
                c0, b0 = SECTIONS[f"KV{layer}"]
                for s in range(4 * BLK):
                    split(c0 + s + AHEAD, (s + AHEAD) % RING)
                    if layer == 0 and s < KT // 2:
                        norm_part(KT // 2 + s, a_hi, 0)
                    if layer == 1 and s in (2, 3):
                        t = s - 2
                        act.wait_ge(h_ready, t + 1)
                        sum_squares(h[:, t, :], ss_h[:, t:t + 1], nat[:, t, :]).then_inc(squares, 1)
                    if layer == 1 and 20 <= s < 20 + KT // 2:
                        norm_part(KT + s - 20, b_hi, 6 * KT)
                    for p in range(2):
                        if s == BLK * (p + 1):
                            n = B_KV[layer] + p
                            if n:
                                act.wait_ge(block_turned, n)
                            if layer and p == 0:
                                act.wait_ge(post_sum, 1)
                            copy_block(c0 + s, (b0 + p) % 2)
                        if s == BLK * (p + 1) + 2:
                            store_half(B_KV[layer] + p, mem_kt[:, 4 * p:4 * p + 2, :])
                    if s == 3 * BLK:
                        store_v(c0 + s, b0 + 2, 0)
                return lambda: store_v(c0 + 4 * BLK, b0 + 3, 1)

            def store_v(c_end, b, i):
                act.wait_ge(chunk_done, c_end)
                if i == 0 and c_end < SECTIONS["RET"][0]:
                    act.wait_ge(tables_ready, 1)
                for t in range(T):
                    last = copy(mem_v[:, t, N * i:N * (i + 1)], acc[:, b % 2, t, :])
                last.then_inc(acc_drained[b % 2], 1)

            def memory(layer):
                c0, b0 = SECTIONS[f"MEM{layer}"]
                for s in range(4 * BLK):
                    split(c0 + s + AHEAD, (s + AHEAD) % RING)
                    if layer == 1 and s == 0:
                        act.wait_ge(chunk_done, c0)
                        act.wait_ge(block_turned, B_SHARED)
                        par = (b0 - 1) % 2
                        kw = KV_HEADS * SWA_DIM
                        for t in range(T):
                            k = acc[:, par, t, 0:kw].rearrange("p (h a d) -> p h a d", h=KV_HEADS, a=1)
                            for dup in range(2):
                                copy(block[:, t, :].rearrange("p (h a d) -> p h a d", h=KV_HEADS, a=2)[:, :, dup:dup + 1, :], k)
                            last = copy(shared_v[:, t, :], acc[:, par, t, kw:2 * kw])
                        last.then_inc(acc_drained[par], 1)
                    if layer == 1 and s == 4:
                        store_half(B_SHARED, shared_kt[:, 0:2, :])
                    for p in range(2):
                        n, u, x = B_MEM[layer] + p, U_MEM[layer] + p, X_MEM[layer] + p
                        if s == 8 + BLK * p:
                            act.wait_ge(block_turned, n)
                            copy_block(c0 + s, (b0 + p) % 2)
                        if s == 10 + BLK * p:
                            if u:
                                act.wait_ge(score_full, u)
                            store_half(n, q_t[:, 0:2, :])
                        if s == 12 + BLK * p:
                            act.wait_ge(neg_ready, x + 1)
                            if x:
                                act.wait_ge(probs_turned, x)
                            for t in range(T):
                                for j in range(2):
                                    last = nc.scalar.activation(
                                        mem_p[:, t, j, :], score[t][:, S * j:S * (j + 1)], ACT.Exp,
                                        bias=neg[:, t, j:j + 1], scale=RET_DIM ** -0.5, accum_out=den[:, t, j:j + 1])
                            last.then_inc(probs_ready, 1)
                        if s == 15 + BLK * p:
                            act.wait_ge(probs_turned, x + 1)
                            if u:
                                act.wait_ge(o_full, u)
                            copy(mem_pt[:, 0], turn[0]).then_inc(probs_a, 1)
                    if s == 24:
                        tanh_gate(GROUPS * layer, c0 + s, b0 % 2)
                    if s == 27:
                        mix_part(GROUPS * layer, 0)
                tanh_gate(GROUPS * layer + 1, c0 + 4 * BLK, (b0 + 1) % 2)

            finish_v = kv(0)
            finish_v()
            memory(0)

            c0, b0 = SECTIONS["RET"]
            with act.Fori(0, 4) as it:
                for s in range(4 * BLK):
                    split(it * (4 * BLK) + (c0 + s + AHEAD), (s + AHEAD) % RING)
                    if s == 3:
                        mix_part(it + 1, it + 1)
                    if s == 12:
                        act.wait_ge(score_full, it + U_RET)
                        store_half(it * 2 + B_RET, q_t[:, 0:2, :])
                    if s == 20:
                        store_half(it * 2 + (B_RET + 1), k_t[:, 0:2, :])
                    if s == 24:
                        act.wait_ge(chunk_done, it * (4 * BLK) + (c0 + s))
                        act.wait_ge(o_full, it + U_RET)
                        for t in range(T):
                            last = copy(v_nat[:, t, :], acc[:, (b0 + 2) % 2, t, :])
                        last.then_inc(acc_drained[(b0 + 2) % 2], 1)
                    if s == 26:
                        act.wait_ge(o_full, it + (U_RET + 1))
                        act.wait_ge(gated_ready, it + 2)
                        for t in range(T):
                            for j in range(2):
                                sum_squares(score[t][:, RET_DIM * j:RET_DIM * (j + 1)], ss_ret[:, 2 * t + j:2 * t + j + 1],
                                            junk[:, (2 * t + j) * RET_DIM:(2 * t + j + 1) * RET_DIM]).then_inc(squares, 1)
                act.wait_ge(squares, it * 4 + 8)
                tanh_gate(it + 2, it * (4 * BLK) + (c0 + 4 * BLK), (b0 + 3) % 2)

            def out_pass(layer, it):
                c0, b0 = SECTIONS[f"OUT{layer}"]
                for b in range(2):
                    for i in range(OBLK):
                        s = OBLK * b + i
                        split(it * (2 * OBLK) + (c0 + s + AHEAD), (s + AHEAD) % RING)
                        if s == OBLK:
                            out_part(layer, it, 0, c0, b0)
                        if layer == 0 and s in (8, 11, 14, 17):
                            g = (s - 8) // 3
                            act.wait_ge(tile_turned, it * 4 + (g + 1))
                            for j in range(4):
                                k = 4 * g + j
                                last = copy(a_hi[:, k, bass.ds(it * P, P)], aux[:, g, P * j:P * (j + 1)],
                                            scale=gains[:, 3 * KT + k:3 * KT + k + 1])
                            last.then_inc(tile_hi, 1)
                out_part(layer, it, 1, c0, b0)

            def out_part(layer, it, b, c0, b0):
                act.wait_ge(chunk_done, it * (2 * OBLK) + (c0 + OBLK * (b + 1)))
                if not (isinstance(it, int) and it + b + layer == 0):
                    act.wait_ge(out_squares, it * 4 + (8 * layer + 2 * b))
                for t in range(T):
                    sum_squares(acc[:, (b0 + b) % 2, t, :], ss_out[:, t, bass.ds(it * 2 + b, 1)],
                                junk[:, N * t:N * (t + 1)]).then_inc(out_squares, 1)

            mix_part(GROUPS - 1, GROUPS - 1)
            with act.Fori(0, 2) as it:
                out_pass(0, it)
            finish_v = kv(1)
            for s in range(BLK):
                split(SECTIONS["SHARED"][0] + s + AHEAD, (s + AHEAD) % RING)
                if s == 0:
                    finish_v()
                norm_part(3 * KT // 2 + s, a_hi, KT)
            memory(1)

            c0, b0 = SECTIONS["SWA"]
            with act.Fori(0, 2) as it:
                c_it = it * (4 * BLK)
                for s in range(4 * BLK):
                    split(c_it + (c0 + s + AHEAD), (s + AHEAD) % RING)
                    if s == 3:
                        mix_part(it * 2 + (GROUPS + 1), it * 2 + 1)
                    for p in range(2):
                        if s == 8 + BLK * p:
                            act.wait_ge(block_turned, it * 2 + (B_SWA + p))
                            copy_block(c_it + (c0 + s), (b0 + p) % 2)
                        if s == 10 + BLK * p:
                            act.wait_ge(score_full, it * (2 * UNITS) + (U_SWA + UNITS * p))
                            store_half(it * 2 + (B_SWA + p), q_t[:, 0:2, :])
                    for p, u in units_at(s, 1):
                        x = it * (2 * UNITS) + (X_SWA + UNITS * p + u)
                        r = u % 2
                        act.wait_ge(neg_ready, x + 1)
                        for e in range(2):
                            for j, (lo, hi) in enumerate(((0, P), (P, 3 * P))):
                                nc.scalar.activation(swa_p[:, r, e, lo:hi], swa_p[:, r, e, lo:hi], ACT.Exp,
                                                     bias=swa_neg[r][:, e, j:j + 1], scale=SWA_DIM ** -0.5,
                                                     accum_out=swa_den[r][:, e, j:j + 1])
                            last = nc.scalar.activation(swa_es[r][:, e, :], swa_neg[r][:, e, :], ACT.Exp,
                                                        bias=sink_cols[:, bass.ds(it * 16 + (8 * p + 2 * u + e), 1)])
                        last.then_inc(probs_ready, 1)
                    for p, u in units_at(s, 4):
                        x = it * (2 * UNITS) + (X_SWA + UNITS * p + u)
                        act.wait_ge(probs_turned, x + 1)
                        act.wait_ge(o_full, it * (2 * UNITS) + (U_SWA + UNITS * p + u - 1))
                        copy(swa_pt[:, u % 2, 0, :], turn[0][:, 0:3 * P]).then_inc(probs_a, 1)
                    if s == 24:
                        tanh_gate(it * 2 + (GROUPS + 2), c_it + (c0 + s), b0 % 2)
                    if s == 28:
                        mix_part(it * 2 + (GROUPS + 2), it * 2 + 2)
                tanh_gate(it * 2 + (GROUPS + 3), c_it + (c0 + 4 * BLK), (b0 + 1) % 2)

            mix_part(2 * GROUPS - 1, GROUPS - 1)
            for it in range(2):
                out_pass(1, it)

        @blk.vector
        def _(dve):
            n_steps = Count()

            def step(ins):
                ins.then_inc(dve_step, 1)
                dve.wait_ge(dve_step, n_steps.up())

            def split(c, slot):
                if isinstance(c, int) and c >= CHUNKS:
                    return
                dve.wait_ge(hi_ready, c + 1)
                dve.tensor_tensor(weight_lo[:, slot], raw[:, slot], weight_hi[:, slot].bitcast(F32),
                                  ALU.subtract).then_inc(lo_ready, 1)

            def norm_part(g, dst_hi, dst_lo, gain):
                dve.wait_ge(norm_hi, g + 1)
                i = g % (KT // 2)
                for j in range(2):
                    k = 2 * i + j
                    last = dve.scalar_tensor_tensor(dst_lo[:, k, :], aux[:, g % 4, S * j:S * (j + 1)],
                                                    gains[:, gain + k:gain + k + 1],
                                                    dst_hi[:, k, :].bitcast(F32), ALU.mult, ALU.subtract)
                last.then_inc(norm_lo, 1)

            def store_half(n, dst):
                dve.wait_ge(block_turned, n + 1)
                dve.tensor_copy(dst, turn[1]).then_inc(block_b, 1)

            def mix_part(g, pos):
                dve.wait_ge(mix_hi, g * 2 + 2)
                for i in range(2):
                    at = bass.ds(pos * 4 + 2 * i, 2)
                    last = dve.tensor_tensor(b_lo[:, at, :], turn[i], b_hi[:, at, :].bitcast(F32), ALU.subtract)
                last.then_inc(mix_lo, 1)

            def gate_group(g, dst, par, drains):
                for t in range(T):
                    dve.wait_ge(tanh_ready, g * 2 + (t + 1))
                    last = dve.scalar_tensor_tensor(gate[:, t, :], gate[:, t, :], 1.0, acc[:, par, t, :],
                                                    ALU.add, ALU.mult)
                last.then_inc(acc_drained[par], 1)
                dve.wait_ge(acc_drained[par], drains)
                dve.tensor_tensor(dst, dst, gate, ALU.mult).then_inc(gated_ready, 1)

            def rope_window(n):
                for t in range(T):
                    v = block[:, t, :].rearrange("p (h d) -> p h d", d=SWA_DIM)
                    x1, x2 = v[:, :, 0:RH], v[:, :, RH:ROT]
                    heads = N // SWA_DIM
                    cos, sin = (f[:, t, :].unsqueeze(1).to_broadcast([P, heads, RH]) for f in (swa_cos, swa_sin))
                    xs = [(rope_a, rope_b)[t][:, heads * RH * i:heads * RH * (i + 1)].rearrange("p (h d) -> p h d", h=heads) for i in range(4)]
                    dve.tensor_tensor(xs[0], x1, cos, ALU.mult)
                    dve.tensor_tensor(xs[1], x2, sin, ALU.mult)
                    dve.tensor_tensor(xs[2], x2, cos, ALU.mult)
                    step(dve.tensor_tensor(xs[3], x1, sin, ALU.mult))
                    dve.tensor_tensor(x1, xs[0], xs[1], ALU.subtract)
                    last = dve.tensor_tensor(x2, xs[2], xs[3], ALU.add)
                last.then_inc(roped, 1)

            dve.wait_ge(pos_in, 16)
            dve.wait_ge(freq_in, 16)
            step(dve.tensor_copy(pos_f, pos_i[:, :]))
            for t in range(T):
                last = dve.tensor_scalar(angle[:, t, :], freq, pos_f[:, t:t + 1], None, ALU.mult)
            last.then_inc(freq_read, 1)
            dve.wait_ge(freq_read, 1)
            for arg, quarter in ((cos_arg, 0.25), (sin_arg, 0.0)):
                step(dve.tensor_scalar(turns, angle, 1.0 / TWO_PI, quarter, ALU.mult, ALU.add))
                step(dve.tensor_scalar(turns, turns, ROUND, -ROUND, ALU.add, ALU.add))
                step(dve.scalar_tensor_tensor(arg, turns, -TWO_PI_1, angle, ALU.mult, ALU.add))
                step(dve.scalar_tensor_tensor(arg, turns, -TWO_PI_2, arg, ALU.mult, ALU.add))
                step(dve.scalar_tensor_tensor(arg, turns, -TWO_PI_3, arg, ALU.mult, ALU.add))
                step(dve.tensor_scalar(arg, arg, quarter * TWO_PI, None, ALU.add))
                step(dve.tensor_scalar(over, arg, PI, -TWO_PI, ALU.is_gt, ALU.mult))
                step(dve.tensor_tensor(arg, arg, over, ALU.add))
                step(dve.tensor_scalar(over, arg, -PI, TWO_PI, ALU.is_lt, ALU.mult))
                step(dve.tensor_tensor(arg, arg, over, ALU.add))
                dve.tensor_scalar(arg, arg, PI_DOWN, -PI_DOWN, ALU.min, ALU.max).then_inc(angles_ready, 1)
            dve.wait_ge(sinks_in, 16)
            dve.tensor_scalar(neg_sinks[:, :], sink_cols[:, :], -1.0, None, ALU.mult)
            dve.wait_ge(gains_turned, 1)
            dve.tensor_copy(gains[:, :], turn[0][:, 0:P]).then_inc(gains_ready, 1)
            dve.wait_ge(rsqrt_ready, R_MEM)
            for t in range(T):
                dve.tensor_scalar(nat[:, t, :], nat[:, t, :], rs_mem[:, t:t + 1], None, ALU.mult).then_inc(normed, 1)
            dve.wait_ge(rsqrt_ready, R_X)
            for t in range(T):
                dve.tensor_scalar(x_nat[:, t, :], h[:, t, :], rs_x[:, t:t + 1], None, ALU.mult).then_inc(normed, 1)
            for c in range(AHEAD):
                split(c, c)
            for g in range(KT // 2):
                norm_part(g, b_hi, b_lo, 2 * KT)

            def kv(layer):
                c0, b0 = SECTIONS[f"KV{layer}"]
                for s in range(4 * BLK):
                    split(c0 + s + AHEAD, (s + AHEAD) % RING)
                    if layer == 0 and s < KT // 2:
                        norm_part(KT // 2 + s, a_hi, a_lo, 0)
                    if layer == 1 and s == 0:
                        post_total(0)
                    if layer == 1 and s in (1, 2):
                        t = s - 1
                        dve.wait_ge(rsqrt_ready, R_POST0)
                        dve.scalar_tensor_tensor(h[:, t, :], nat[:, t, :], rs_post[:, t:t + 1], h[:, t, :],
                                                 ALU.mult, ALU.add).then_inc(h_ready, 1)
                    if layer == 1 and s in (5, 6):
                        t = s - 5
                        dve.wait_ge(rsqrt_ready, R_H)
                        dve.tensor_scalar(nat[:, t, :], h[:, t, :], rs_h[:, t:t + 1], None, ALU.mult).then_inc(normed, 1)
                    if layer == 1 and 20 <= s < 20 + KT // 2:
                        norm_part(KT + s - 20, b_hi, b_lo, 6 * KT)
                    for p in range(2):
                        if s == BLK * (p + 1) + 2:
                            store_half(B_KV[layer] + p, mem_kt[:, 4 * p + 2:4 * p + 4, :])

            def memory(layer):
                c0, b0 = SECTIONS[f"MEM{layer}"]
                for s in range(4 * BLK):
                    split(c0 + s + AHEAD, (s + AHEAD) % RING)
                    if layer == 1 and s == 1:
                        drained(dve, b0 - 1)
                        rope_window(ROPE_SHARED)
                    if layer == 1 and s == 4:
                        store_half(B_SHARED, shared_kt[:, 2:4, :])
                    for p in range(2):
                        n, u, x = B_MEM[layer] + p, U_MEM[layer] + p, X_MEM[layer] + p
                        if s == 10 + BLK * p:
                            if u:
                                dve.wait_ge(score_full, u)
                            store_half(n, q_t[:, 2:4, :])
                        if s == 12 + BLK * p:
                            dve.wait_ge(score_full, u + 1)
                            for t in range(T):
                                last = dve.tensor_reduce(top[:, t, :], score[t].rearrange("p (h m) -> p h m", h=2),
                                                         AX.X, ALU.max)
                            step(last)
                            dve.tensor_scalar(neg, top, -RET_DIM ** -0.5, None, ALU.mult).then_inc(neg_ready, 1)
                        if s == 15 + BLK * p:
                            dve.wait_ge(probs_turned, x + 1)
                            if u:
                                dve.wait_ge(o_full, u)
                            dve.reciprocal(inv, den)
                            dve.tensor_copy(mem_pt[:, 1], turn[1]).then_inc(probs_b, 1)
                            dve.wait_ge(probs_b, x + 1)
                        if s == 17 + BLK * p:
                            dve.wait_ge(o_full, u + 1)
                            store_o(p, [inv[:, t, :] for t in range(T)])
                    if s == 25:
                        gate_group(GROUPS * layer, gated[0], b0 % 2, (b0 + 2) // 2 + 1)
                    if s == 27:
                        mix_part(GROUPS * layer, 0)
                gate_group(GROUPS * layer + 1, gated[1], (b0 + 1) % 2, (b0 + 3) // 2 + 1)

            def store_o(i, factors, scale=0.5):
                for t in range(T):
                    o = score[t].rearrange("p (h d) -> p h d", h=2)
                    last = dve.scalar_tensor_tensor(gated[i][:, t, :].rearrange("p (h d) -> p h d", h=2), o, scale,
                                                    factors[t].unsqueeze(2).to_broadcast([P, 2, RET_DIM]),
                                                    ALU.mult, ALU.mult)
                last.then_inc(o_stored, 1)

            def post_total(layer):
                dve.wait_ge(out_squares, 8 * (layer + 1))
                dve.tensor_reduce(ss_post, ss_out, AX.X, ALU.add).then_inc(post_sum, 1)

            kv(0)
            memory(0)

            c0, b0 = SECTIONS["RET"]
            with dve.Fori(0, 4) as it:
                n_steps.enter(it, 4)
                for s in range(4 * BLK):
                    split(it * (4 * BLK) + (c0 + s + AHEAD), (s + AHEAD) % RING)
                    if s == 3:
                        mix_part(it + 1, it + 1)
                    for j in range(2):
                        if s == 8 + BLK * j:
                            par = (b0 + j) % 2
                            dve.wait_ge(chunk_done, it * (4 * BLK) + (c0 + s))
                            dve.wait_ge(block_turned, it * 2 + (B_RET + j))
                            if j == 0:
                                dve.wait_ge(tables_ready, 1)
                            for t in range(T):
                                z = acc[:, par, t, :].rearrange("p (a f) -> p a f", f=HALF)
                                zh = acc[:, par, t, :].rearrange("p (h a f) -> p h a f", h=2, a=2)
                                ra = rope_a.rearrange("p (a f) -> p a f", f=HALF)
                                ah, bh, oh = (v.rearrange("p (h a f) -> p h a f", h=2, a=2)
                                              for v in (rope_a, rope_b, block[:, t, :]))
                                cos = ret_cos[:, t, :].unsqueeze(1).to_broadcast([P, 4, HALF])
                                sin = ret_sin[:, t, :].unsqueeze(1).to_broadcast([P, 2, HALF])
                                dve.tensor_tensor(ra, z, cos, ALU.mult)
                                dve.tensor_tensor(bh[:, :, 0, :], zh[:, :, 1, :], sin, ALU.mult)
                                last = dve.tensor_tensor(bh[:, :, 1, :], zh[:, :, 0, :], sin, ALU.mult)
                                if t == 0:
                                    step(last)
                                else:
                                    last.then_inc(acc_drained[par], 1)
                                    drained(dve, b0 + j, it, 4)
                                dve.tensor_tensor(oh[:, :, 0, :], ah[:, :, 0, :], bh[:, :, 0, :], ALU.subtract)
                                last = dve.tensor_tensor(oh[:, :, 1, :], ah[:, :, 1, :], bh[:, :, 1, :], ALU.add)
                                if t == 0:
                                    step(last)
                            last.then_inc(roped, 1)
                    if s == 12:
                        dve.wait_ge(score_full, it + U_RET)
                        store_half(it * 2 + B_RET, q_t[:, 2:4, :])
                    if s == 20:
                        store_half(it * 2 + (B_RET + 1), k_t[:, 2:4, :])
                    if s == 23:
                        dve.wait_ge(score_full, it + (U_RET + 1))
                        dve.wait_ge(decay_in, it * 16 + 16)
                        dve.wait_ge(o_full, it + U_RET)
                        for j in range(2):
                            last = dve.tensor_tensor(masked[:, j, :], score[j][:, 0:3 * P], decay[:, j, :], ALU.mult)
                        last.then_inc(masked_ready, 1)
                    if s == 27:
                        dve.wait_ge(rsqrt_ready, it + R_RET)
                        dve.wait_ge(gated_turned, it + 2)
                        store_o(1, [rs_ret[:, 2 * t:2 * t + 2] for t in range(T)], RET_DIM ** 0.5 / 2)
                gate_group(it + 2, gated[1], (b0 + 3) % 2, it * 2 + ((b0 + 3) // 2 + 1))
            n_steps.leave(4)

            def out_pass(layer, it):
                c0, b0 = SECTIONS[f"OUT{layer}"]
                for b in range(2):
                    for i in range(OBLK):
                        s = OBLK * b + i
                        split(it * (2 * OBLK) + (c0 + s + AHEAD), (s + AHEAD) % RING)
                        if layer == 0 and s == 4:
                            dve.wait_ge(mem_tile_in, it * 16 + 16)
                            dve.tensor_scalar(mem_tile, mem_tile, rs_mem[:, bass.ds(it, 1)], None,
                                              ALU.mult).then_inc(tile_normed, 1)
                        if s == OBLK:
                            out_part(layer, it, 0, b0)
                        if layer == 0 and s in (8, 11, 14, 17):
                            g = (s - 8) // 3
                            dve.wait_ge(tile_hi, it * 4 + (g + 1))
                            for j in range(4):
                                k = 4 * g + j
                                at = bass.ds(it * P, P)
                                last = dve.scalar_tensor_tensor(a_lo[:, k, at], aux[:, g, P * j:P * (j + 1)],
                                                                gains[:, 3 * KT + k:3 * KT + k + 1],
                                                                a_hi[:, k, at].bitcast(F32), ALU.mult, ALU.subtract)
                            last.then_inc(tile_lo, 1)
                out_part(layer, it, 1, b0)

            def out_part(layer, it, b, b0):
                par = (b0 + b) % 2
                dve.wait_ge(out_squares, it * 4 + (8 * layer + 2 * b + 2))
                dve.wait_ge(post_in, 16 * (layer + 1))
                at = bass.ds(it * (2 * N) + N * b, N)
                for t in range(T):
                    last = dve.tensor_tensor(nat[:, t, at], acc[:, par, t, :], post_gain[:, at], ALU.mult)
                last.then_inc(acc_drained[par], 1)

            mix_part(GROUPS - 1, GROUPS - 1)
            with dve.Fori(0, 2) as it:
                out_pass(0, it)
            drained(dve, SECTIONS["OUT0"][1] + 2)
            drained(dve, SECTIONS["OUT0"][1] + 3)
            kv(1)
            for s in range(BLK):
                split(SECTIONS["SHARED"][0] + s + AHEAD, (s + AHEAD) % RING)
                norm_part(3 * KT // 2 + s, a_hi, a_lo, KT)
            memory(1)

            dve.wait_ge(band_in, 16)
            c0, b0 = SECTIONS["SWA"]
            with dve.Fori(0, 2) as it:
                n_steps.enter(it, 2 * (T + 4 * UNITS))
                for s in range(4 * BLK):
                    split(it * (4 * BLK) + (c0 + s + AHEAD), (s + AHEAD) % RING)
                    if s == 3:
                        mix_part(it * 2 + (GROUPS + 1), it * 2 + 1)
                    for p in range(2):
                        if s == 8 + BLK * p:
                            drained(dve, b0 + p, it, 4)
                            rope_window(it * 2 + (ROPE_SWA + p))
                        if s == 10 + BLK * p:
                            dve.wait_ge(score_full, it * (2 * UNITS) + (U_SWA + UNITS * p))
                            store_half(it * 2 + (B_SWA + p), q_t[:, 2:4, :])
                    for p, u in units_at(s, 1):
                        un = it * (2 * UNITS) + (U_SWA + UNITS * p + u)
                        x = it * (2 * UNITS) + (X_SWA + UNITS * p + u)
                        r = u % 2
                        dve.wait_ge(score_full, un + 1)
                        dve.wait_ge(probs_turned, x - 1)
                        dve.tensor_tensor(swa_p[:, r, 0, 0:P], score[0][:, 0:P], band[:, 0:P], ALU.add)
                        for e, j, lo, hi in ((0, 1, P, 3 * P), (1, 0, 0, P), (1, 1, P, 3 * P)):
                            last = dve.tensor_tensor_reduce(
                                swa_p[:, r, e, lo:hi], score[e][:, lo:hi], band[:, lo:hi], 1.0, -3e38,
                                ALU.add, ALU.max, swa_top[r][:, e, j:j + 1])
                        step(last)
                        step(dve.tensor_reduce(swa_top[r][:, 0, 0:1], swa_p[:, r, 0, 0:P], AX.X, ALU.max))
                        for e in range(2):
                            last = dve.tensor_scalar(swa_neg[r][:, e, :], swa_top[r][:, e, :], -SWA_DIM ** -0.5,
                                                     neg_sinks[:, bass.ds(it * 16 + (8 * p + 2 * u + e), 1)],
                                                     ALU.mult, ALU.min)
                        last.then_inc(neg_ready, 1)
                    for p, u in units_at(s, 6):
                        un = it * (2 * UNITS) + (U_SWA + UNITS * p + u)
                        dve.wait_ge(o_full, un + 1)
                        dve.wait_ge(gated_turned, it * 2 + (GROUPS + 1 + p))
                        for e in range(2):
                            col = (2 * u + e) * SWA_DIM
                            last = dve.scalar_tensor_tensor(
                                gated[p][:, :, col:col + SWA_DIM],
                                score[e][:, 3 * P:N].rearrange("p (t d) -> p t d", t=T), 0.5,
                                swa_inv[u % 2][:, e, :].unsqueeze(2).to_broadcast([P, T, SWA_DIM]),
                                ALU.mult, ALU.mult)
                        last.then_inc(o_stored, 1)
                    for p, u in units_at(s, 2):
                        r = u % 2
                        dve.wait_ge(probs_ready, it * (2 * UNITS) + (X_SWA + UNITS * p + u + 1))
                        dve.wait_ge(o_stored, it * (2 * UNITS) + (U_SWA + UNITS * p + u - 1))
                        step(dve.tensor_tensor(swa_den[r], swa_den[r], swa_es[r], ALU.add))
                        step(dve.reciprocal(swa_inv[r], swa_den[r]))
                    for p, u in units_at(s, 4):
                        x = it * (2 * UNITS) + (X_SWA + UNITS * p + u)
                        dve.wait_ge(probs_turned, x + 1)
                        dve.wait_ge(o_full, it * (2 * UNITS) + (U_SWA + UNITS * p + u - 1))
                        dve.tensor_copy(swa_pt[:, u % 2, 1, :], turn[1][:, 0:3 * P]).then_inc(probs_b, 1)
                    if s == 25:
                        dve.wait_ge(o_stored, it * (2 * UNITS) + (U_SWA + UNITS))
                        gate_group(it * 2 + (GROUPS + 2), gated[0], b0 % 2, it * 2 + ((b0 + 2) // 2 + 1))
                    if s == 28:
                        mix_part(it * 2 + (GROUPS + 2), it * 2 + 2)
                dve.wait_ge(o_stored, it * (2 * UNITS) + (U_SWA + 2 * UNITS))
                gate_group(it * 2 + (GROUPS + 3), gated[1], (b0 + 1) % 2, it * 2 + ((b0 + 3) // 2 + 1))
            n_steps.leave(2)

            mix_part(2 * GROUPS - 1, GROUPS - 1)
            for it in range(2):
                out_pass(1, it)
            drained(dve, SECTIONS["OUT1"][1] + 2)
            drained(dve, SECTIONS["OUT1"][1] + 3)
            post_total(1)
            dve.wait_ge(rsqrt_ready, R_POST1)
            for t in range(T):
                dve.scalar_tensor_tensor(nat[:, t, :], nat[:, t, :], rs_post[:, t:t + 1], h[:, t, :],
                                         ALU.mult, ALU.add).then_inc(final_ready, 1)

        @blk.tensor
        def _(pe):
            def chunk(c, slot, par, i, blocks, hi, lo):
                pe.wait_ge(lo_ready, c + 1)
                for j in range(CK):
                    k = CK * i + j
                    for t in range(T):
                        tok = slice(t * P, (t + 1) * P)
                        first, last = i == 0 and j == 0, i == blocks - 1 and j == CK - 1
                        o = acc[:, par, t, :]
                        pe.matmul(o, hi[:, k, tok], weight_hi[:, slot, j, :], start=first, stop=False)
                        pe.matmul(o, hi[:, k, tok], weight_lo[:, slot, j, :], start=False, stop=False)
                        mm = pe.matmul(o, lo[:, k, tok], weight_hi[:, slot, j, :], start=False, stop=last)
                mm.then_inc(chunk_done, 1)

            def free_acc(b, it=0, per=0):
                if b >= 2:
                    pe.wait_ge(acc_drained[b % 2], it * (per // 2) + b // 2)

            def norm_group(g, src):
                if g >= 4:
                    pe.wait_ge(norm_lo, g - 3)
                i = g % (KT // 2)
                for j in range(2):
                    for t in range(T):
                        mm = pe.transpose(aux[:, g % 4, S * j + P * t:S * j + P * (t + 1)],
                                          src[:, t, (2 * i + j) * P:(2 * i + j + 1) * P], ident[:, :])
                mm.then_inc(norm_turned, 1)

            def turn_natural(src, sem_turned):
                for i in range(4):
                    for t in range(T):
                        mm = pe.transpose(turn[i // 2][:, (i % 2) * S + t * P:(i % 2) * S + (t + 1) * P],
                                          src[:, t, i * P:(i + 1) * P], ident[:, :])
                mm.then_inc(sem_turned, 1)

            def stored(n):
                if not (isinstance(n, int) and n == 0):
                    pe.wait_ge(block_a, n)
                    pe.wait_ge(block_b, n)

            def turn_gated(g, i, mixed):
                pe.wait_ge(gated_ready, g + 1)
                if not (isinstance(mixed, int) and mixed == 0):
                    pe.wait_ge(mix_lo, mixed)
                turn_natural(gated[i], gated_turned)

            pe.wait_ge(ident_in, 16)
            pe.wait_ge(gains_in, 16 * 5)
            pe.transpose(turn[0][:, 0:P], gain_rows, ident[:, :]).then_inc(gains_turned, 1)
            pe.wait_ge(gains_ready, 1)
            pe.wait_ge(normed, 2)
            for g in range(KT // 2):
                norm_group(g, nat)
            pe.wait_ge(normed, 4)

            def kv(layer):
                c0, b0 = SECTIONS[f"KV{layer}"]
                src = (b_hi, b_lo) if layer == 0 else (a_hi, a_lo)
                for s in range(4 * BLK):
                    b, i = divmod(s, BLK)
                    if i == 0:
                        free_acc(b0 + b)
                    if s < KT // 2:
                        if layer == 0:
                            pe.wait_ge(norm_lo, s + 1)
                        else:
                            pe.wait_ge(tile_lo, 8)
                    chunk(c0 + s, s % RING, (b0 + b) % 2, i, BLK, *src)
                    if layer == 0 and s < KT // 2:
                        norm_group(KT // 2 + s, x_nat)
                    if layer == 1 and 20 <= s < 20 + KT // 2:
                        pe.wait_ge(normed, 6)
                        stored(B_KV[1] + 2)
                        norm_group(KT + s - 20, nat)
                    for p in range(2):
                        if s == BLK * (p + 1) + 1:
                            n = B_KV[layer] + p
                            drained(pe, b0 + p)
                            stored(n)
                            if layer == 0:
                                pe.wait_ge(norm_lo, KT)
                            turn_natural(block, block_turned)

            def memory(layer):
                c0, b0 = SECTIONS[f"MEM{layer}"]
                for s in range(4 * BLK):
                    b, i = divmod(s, BLK)
                    if i == 0:
                        free_acc(b0 + b)
                    if s == 0:
                        pe.wait_ge(norm_lo, KT if layer == 0 else 2 * KT)
                    chunk(c0 + s, s % RING, (b0 + b) % 2, i, BLK, a_hi, a_lo)
                    if layer == 1 and s == 3:
                        pe.wait_ge(roped, ROPE_SHARED + 1)
                        turn_natural(block, block_turned)
                    for p in range(2):
                        n, u, x = B_MEM[layer] + p, U_MEM[layer] + p, X_MEM[layer] + p
                        if s == 9 + BLK * p:
                            drained(pe, b0 + p)
                            stored(n)
                            if x:
                                pe.wait_ge(probs_a, x)
                                pe.wait_ge(probs_b, x)
                            turn_natural(block, block_turned)
                        if s == 11 + BLK * p:
                            stored(n + 1)
                            if u:
                                pe.wait_ge(o_stored, u)
                            for t in range(T):
                                for j in range(2):
                                    for d in range(2):
                                        mm = pe.matmul(score[t][:, S * j:S * (j + 1)], q_t[:, 2 * j + d, t * P:(t + 1) * P],
                                                       mem_kt[:, 4 * p + 2 * j + d, :], start=(d == 0), stop=(d == 1))
                            mm.then_inc(score_full, 1)
                        if s == 14 + BLK * p:
                            pe.wait_ge(probs_ready, x + 1)
                            for j in range(2):
                                for m in range(2):
                                    for t in range(T):
                                        mm = pe.transpose(turn[j][:, m * S + t * P:m * S + (t + 1) * P],
                                                          mem_p[:, t, j, m * P:(m + 1) * P], ident[:, :])
                            mm.then_inc(probs_turned, 1)
                        if s == 16 + BLK * p:
                            pe.wait_ge(probs_a, x + 1)
                            pe.wait_ge(probs_b, x + 1)
                            drained(pe, SECTIONS[f"KV{layer}"][1] + 2 + p)
                            for t in range(T):
                                for j in range(2):
                                    for m in range(2):
                                        mm = pe.matmul(score[t][:, RET_DIM * j:RET_DIM * (j + 1)],
                                                       mem_pt[:, j, m, t * P:(t + 1) * P],
                                                       mem_v[:, m, (2 * p + j) * RET_DIM:(2 * p + j + 1) * RET_DIM],
                                                       start=(m == 0), stop=(m == 1))
                            mm.then_inc(o_full, 1)
                    if s == 26:
                        turn_gated(GROUPS * layer, 0, GROUPS * layer)

            kv(0)
            memory(0)

            c0, b0 = SECTIONS["RET"]
            with pe.Fori(0, 4) as it:
                for s in range(4 * BLK):
                    b, i = divmod(s, BLK)
                    if i == 0:
                        free_acc(b0 + b, it, 4)
                    chunk(it * (4 * BLK) + (c0 + s), s % RING, (b0 + b) % 2, i, BLK, a_hi, a_lo)
                    if s == 2:
                        turn_gated(it + 1, 1, it + 1)
                    for j in range(2):
                        if s == 11 + BLK * j:
                            pe.wait_ge(roped, it * 2 + (ROPE_RET + j + 1))
                            stored(it * 2 + (B_RET + j))
                            if j == 0:
                                pe.wait_ge(mix_lo, it + 2)
                            turn_natural(block, block_turned)
                    if s == 22:
                        stored(it * 2 + (B_RET + 2))
                        pe.wait_ge(o_stored, it + U_RET)
                        for j in range(2):
                            for q0, q1, k0, c in ((0, S, 0, 0), (P, S, P, S)):
                                for d in range(2):
                                    mm = pe.matmul(score[j][:, c:c + q1 - q0], k_t[:, 2 * j + d, k0:k0 + P],
                                                   q_t[:, 2 * j + d, q0:q1], start=(d == 0), stop=(d == 1))
                        mm.then_inc(score_full, 1)
                    if s == 25:
                        pe.wait_ge(masked_ready, it + 1)
                        drained(pe, b0 + 2, it, 4)
                        for t in range(T):
                            for j in range(2):
                                cols = slice(RET_DIM * j, RET_DIM * (j + 1))
                                for m in range(t + 1):
                                    at = m * S + (t - m) * P
                                    mm = pe.matmul(score[t][:, cols], masked[:, j, at:at + P], v_nat[:, m, cols],
                                                   start=(m == 0), stop=(m == t))
                        mm.then_inc(o_full, 1)

            def out_pass(layer, it):
                c0, b0 = SECTIONS[f"OUT{layer}"]
                for b in range(2):
                    for i in range(OBLK):
                        s = OBLK * b + i
                        if i == 0:
                            free_acc(b0 + b, it, 2)
                        chunk(it * (2 * OBLK) + (c0 + s), s % RING, (b0 + b) % 2, i, OBLK, b_hi, b_lo)
                        if layer == 0 and s in (7, 10, 13, 16):
                            g = (s - 7) // 3
                            pe.wait_ge(tile_normed, it + 1)
                            for j in range(4):
                                mm = pe.transpose(aux[:, g, P * j:P * (j + 1)],
                                                  mem_tile[:, (4 * g + j) * P:(4 * g + j + 1) * P], ident[:, :])
                            mm.then_inc(tile_turned, 1)

            turn_gated(GROUPS - 1, 1, GROUPS - 1)
            pe.wait_ge(mix_lo, GROUPS)
            pe.wait_ge(o_stored, U_MEM[1])
            with pe.Fori(0, 2) as it:
                out_pass(0, it)
            kv(1)
            c0, b0 = SECTIONS["SHARED"]
            for s in range(BLK):
                if s == 0:
                    free_acc(b0)
                pe.wait_ge(norm_lo, KT + s + 1)
                chunk(c0 + s, s % RING, b0 % 2, s, BLK, b_hi, b_lo)
                norm_group(3 * KT // 2 + s, nat)
            memory(1)

            c0, b0 = SECTIONS["SWA"]
            with pe.Fori(0, 2) as it:
                for s in range(4 * BLK):
                    b, i = divmod(s, BLK)
                    if i == 0:
                        free_acc(b0 + b, it, 4)
                    chunk(it * (4 * BLK) + (c0 + s), s % RING, (b0 + b) % 2, i, BLK, a_hi, a_lo)
                    if s == 2:
                        turn_gated(it * 2 + (GROUPS + 1), 1, it * 2 + (GROUPS + 1))
                    for p, u in units_at(s, 5):
                        x = it * (2 * UNITS) + (X_SWA + UNITS * p + u)
                        un = it * (2 * UNITS) + (U_SWA + UNITS * p + u)
                        pe.wait_ge(probs_a, x + 1)
                        pe.wait_ge(probs_b, x + 1)
                        pe.wait_ge(o_stored, un)
                        if UNITS * p + u + 2 < 2 * UNITS:
                            pe.wait_ge(neg_ready, x + 3)
                        for e in range(2):
                            for t in range(T):
                                for m in range(t + 1):
                                    at = (t + m) * P
                                    mm = pe.matmul(score[e][:, 3 * P + SWA_DIM * t:3 * P + SWA_DIM * (t + 1)],
                                                   swa_pt[:, u % 2, e, at:at + P],
                                                   swa_v[:, m, p * SWA_DIM:(p + 1) * SWA_DIM],
                                                   start=(m == 0), stop=(m == t))
                        mm.then_inc(o_full, 1)
                    for p, u in units_at(s, 0):
                        x = it * (2 * UNITS) + (X_SWA + UNITS * p + u)
                        if u == 0:
                            stored(it * 2 + (B_SWA + p + 1))
                            pe.wait_ge(copies_ready, it + 1)
                        if (p, u) == (0, 0):
                            pe.wait_ge(o_stored, it * (2 * UNITS) + U_SWA)
                        pe.wait_ge(neg_ready, x)
                        pe.wait_ge(o_stored, it * (2 * UNITS) + (U_SWA + UNITS * p + u - 2))
                        for e in range(2):
                            half = slice(64 * e, 64 * e + 64)
                            pe.matmul(score[e][:, 0:P], q_t[half, u, 0:P], swa_kt[half, p, 0:P], start=True, stop=True)
                            mm = pe.matmul(score[e][:, P:3 * P], q_t[half, u, P:S], swa_kt[half, p, :], start=True, stop=True)
                        mm.then_inc(score_full, 1)
                    for p, u in units_at(s, 3):
                        x = it * (2 * UNITS) + (X_SWA + UNITS * p + u)
                        pe.wait_ge(probs_ready, x + 1)
                        pe.wait_ge(probs_a, x)
                        pe.wait_ge(probs_b, x)
                        if (p, u) == (0, 2):
                            stored(it * 2 + (B_SWA + 2))
                        if (p, u) == (1, 3):
                            pe.wait_ge(mix_lo, it * 2 + (GROUPS + 3))
                        for e in range(2):
                            for j in range(3):
                                mm = pe.transpose(turn[e][:, P * j:P * (j + 1)], swa_p[:, u % 2, e, P * j:P * (j + 1)], ident[:, :])
                        mm.then_inc(probs_turned, 1)
                    for p in range(2):
                        if s == 9 + BLK * p:
                            pe.wait_ge(roped, it * 2 + (ROPE_SWA + p + 1))
                            if p == 0:
                                pe.wait_ge(mix_lo, it * 2 + (GROUPS + 2))
                            pe.wait_ge(probs_a, it * (2 * UNITS) + (X_SWA + 2 * p))
                            pe.wait_ge(probs_b, it * (2 * UNITS) + (X_SWA + 2 * p))
                            turn_natural(block, block_turned)
                    if s == 27:
                        pe.wait_ge(probs_a, it * (2 * UNITS) + (X_SWA + 7))
                        pe.wait_ge(probs_b, it * (2 * UNITS) + (X_SWA + 7))
                        turn_gated(it * 2 + (GROUPS + 2), 0, it * 2 + (GROUPS + 2))
            turn_gated(2 * GROUPS - 1, 1, 2 * GROUPS - 1)
            pe.wait_ge(mix_lo, 2 * GROUPS)
            for it in range(2):
                out_pass(1, it)


def _constants():
    import numpy as np
    ident = np.eye(P, dtype=np.float32)
    ret = np.float32(10000.0) ** (-np.arange(0, RET_DIM, 2, dtype=np.float32) / np.float32(RET_DIM))
    swa = np.float32(500000.0) ** (-np.arange(0, ROT, 2, dtype=np.float32) / np.float32(ROT))
    freq = np.broadcast_to(np.concatenate([ret, swa]).astype(np.float32), (P, FREQS)).copy()
    m, q = np.arange(P)[:, None], np.arange(S)[None, :]
    gamma = np.log1p(-np.exp2(-5.0 - np.arange(RET_HEADS)))
    full = np.where(q >= m, np.exp(gamma[:, None, None] * np.maximum(q - m, 0)), 0.0) * RET_DIM ** -0.5
    decay = np.concatenate([full, full[:, :, 0:P]], axis=2).transpose(1, 0, 2).astype(np.float32).copy()
    q, k = np.arange(P)[:, None], np.arange(P)[None, :]
    own, before = np.where(k <= q, 0.0, -1e30), np.where(k > q, 0.0, -1e30)
    band = np.concatenate([own, before, own], axis=1).astype(np.float32)
    return {"c_ident": ident, "c_freq": freq, "c_decay": decay, "c_band": band}


_INS = ["x", "mem", "positions", "pre_norm_g", "post_norm_g", "mem_norm_g", "kv_norm_g",
        "w_in_a", "w_in_b", "w_kv_b", "sinks_b", "w_mem_kv", "w_out"]


def kernel(**inputs):
    import numpy as np
    from concourse import bacc
    from concourse.bass_utils import run_bass_kernel_spmd

    nc = bacc.Bacc("TRN2", target_bir_lowering=False, num_devices=1)
    arrays = {f"in_{name}": np.ascontiguousarray(inputs[name]) for name in _INS}
    arrays.update(_constants())
    args = [nc.dram_tensor(name, a.shape, mybir.dt.from_np(a.dtype), kind="ExternalInput").ap()
            for name, a in arrays.items()]
    out = nc.dram_tensor("out_h", (1, S, D), F32, kind="ExternalOutput").ap()
    trunk(nc, *args, out)
    result = run_bass_kernel_spmd(nc, [arrays], core_ids=[0])
    return result.results[0]["out_h"]
```

```python
from contextlib import ExitStack

import concourse.bass as bass
from concourse import mybir

F32 = mybir.dt.float32
F32R = mybir.dt.float32r
I32 = mybir.dt.int32
ALU = mybir.AluOpType
ACT = mybir.ActivationFunctionType
AX = mybir.AxisListType

P = 128
S = 256
T = S // P
D = 2048
KT = D // P
N = 512
CK = 2
RING = 4
AHEAD, LO_AHEAD = 3, 2
WARM_UP = 14
RET_HEADS, RET_DIM = 8, 256
SWA_HEADS, SWA_DIM, KV_HEADS, WINDOW = 32, 64, 4, 128
MEM_WIDTH = 1024
MIX = D + MEM_WIDTH
EPS = 1e-6
HALF = RET_DIM // 2
ROT = SWA_DIM // 4
RH = ROT // 2
FREQS = HALF + RH
BLK = KT // CK
OBLK = MIX // P // CK
GAINS = 5 * KT
GROUPS = 6
PIECE, OUT_PIECE = 512, 256

SECTIONS = {}
_c = _b = 0
for _name, _blocks, _len in (("KV0", 4, BLK), ("MEM0", 4, BLK), ("RET", 16, BLK), ("OUT0", 4, OBLK),
                             ("KV1", 4, BLK), ("SHARED", 1, BLK), ("MEM1", 4, BLK), ("SWA", 8, BLK),
                             ("OUT1", 4, OBLK)):
    SECTIONS[_name] = (_c, _b)
    _c += _blocks * _len
    _b += _blocks
CHUNKS = _c

TWO_PI_1 = 6.28125
TWO_PI_2 = 0.0019350051879882812
PI = 3.141592653589793
TWO_PI_3 = 2 * PI - TWO_PI_1 - TWO_PI_2
PI_DOWN = 3.1415925
TWO_PI = 2 * PI
ROUND = 12582912.0


class Count:

    def __init__(self):
        self.n, self.it, self.per, self.start = 0, None, 0, 0

    def enter(self, it, per):
        self.it, self.per, self.start = it, per, self.n

    def leave(self, passes):
        assert self.n - self.start == self.per, (self.n - self.start, self.per)
        self.n, self.it = self.start + self.per * passes, None

    def up(self, k=1):
        self.n += k
        return self.value

    @property
    def value(self):
        return self.n if self.it is None else self.it * self.per + self.n


def trunk(nc, x, mem, positions, pre_g, post_g, mem_g, kv_g, w_in_a, w_in_b, w_kv, sinks, w_mem, w_out,
          c_ident, c_freq, c_decay, c_band, out):
    ctx = ExitStack()
    with ctx:
        def sb(name, shape, dt=F32):
            return ctx.enter_context(nc.sbuf_tensor(name, shape, dt))

        def sem(name):
            return ctx.enter_context(nc.semaphore(name))

        a_hi = sb("a_hi", [P, KT, S], F32R)
        a_lo = sb("a_lo", [P, KT, S], F32R)
        b_hi = sb("b_hi", [P, MIX // P, S], F32R)
        b_lo = sb("b_lo", [P, MIX // P, S], F32R)
        raw = sb("raw", [P, RING, CK, N])
        weight_hi = sb("weight_hi", [P, RING, CK, N], F32R)
        weight_lo = sb("weight_lo", [P, RING, CK, N], F32R)
        h = sb("h", [P, T, D])
        nat = sb("nat", [P, T, D])
        work = sb("work", [P, 5 * 1024])
        mem_kt = sb("mem_kt", [P, MEM_WIDTH // P, S], F32R)
        mem_v = sb("mem_v", [P, T, MEM_WIDTH], F32R)
        shared_kt = sb("shared_kt", [P, KV_HEADS, S])
        shared_v = sb("shared_v", [P, T, KV_HEADS * SWA_DIM])
        swa_cos = sb("swa_cos", [P, T, RH])[:, :, :]
        swa_sin = sb("swa_sin", [P, T, RH])[:, :, :]
        ident = sb("ident", [P, P])
        band = sb("band", [P, 3 * P])
        gains = sb("gains", [P, GAINS])
        sink_cols = sb("sink_cols", [P, SWA_HEADS])
        neg_sinks = sb("neg_sinks", [P, SWA_HEADS])
        stats = sb("stats", [P, 128])
        minus_half = sb("minus_half", [P, 4])
        ret_eps = sb("ret_eps", [P, 4])

        ret_cos = shared_kt[:, 0, :].rearrange("p (t f) -> p t f", t=T)
        ret_sin = shared_kt[:, 1, :].rearrange("p (t f) -> p t f", t=T)
        mem_q_hi, mem_q_lo = b_hi[:, 8:12, :], b_lo[:, 8:12, :]
        mem_pt_hi, mem_pt_lo = b_hi[:, 12:16, :], b_lo[:, 12:16, :]
        mem_kt_lo = b_hi[:, 16:24, :]
        mem_v_lo = b_lo[:, 16:24, :].rearrange("p k s -> p (k s)").rearrange("p (t n) -> p t n", t=T)
        ret_q_hi, ret_q_lo = mem_kt[:, 0:4, :], mem_kt[:, 4:8, :]
        ret_k_hi, ret_k_lo = (mem_v[:, i, :].rearrange("p (k s) -> p k s", k=4) for i in range(T))
        block = work[:, 0:1024].rearrange("p (t n) -> p t n", t=T)
        q_t = work[:, 1024:2048].rearrange("p (k s) -> p k s", k=4)
        gated = [work[:, 2048 + 1024 * i:3072 + 1024 * i].rearrange("p (t n) -> p t n", t=T) for i in range(2)]
        gate = work[:, 4096:5120].rearrange("p (t n) -> p t n", t=T)
        rope_a, rope_b = gate[:, 0, :], gate[:, 1, :]
        squared = work[:, 2048:4096]
        post_gain = work[:, 0:2048]
        mem_tile = work[:, 2048:4096]
        junk = work[:, 4096:5120]
        gain_rows = work[0:GAINS, 4096:4096 + P]
        nat_f = nat[:, :, :].rearrange("p t n -> p (t n)")
        v_nat = nat_f[:, 1024:2048].rearrange("p (t n) -> p t n", t=T)
        masked = nat_f[:, 2048:2816].rearrange("p (h n) -> p h n", h=2)
        decay = nat_f[:, 2816:3584].rearrange("p (h n) -> p h n", h=2)
        mem_p = nat_f[:, 0:1024].rearrange("p (t h m) -> p t h m", t=T, h=2)
        swa_p = nat_f[:, 0:1536].rearrange("p (r e n) -> p r e n", r=2, e=2)
        swa_pt = nat_f[:, 1536:3072].rearrange("p (r e n) -> p r e n", r=2, e=2)
        swa_kt = nat_f[:, 3072:3584].rearrange("p (g s) -> p g s", g=2)
        swa_v = nat_f[:, 3584:3840].rearrange("p (t n) -> p t n", t=T)
        freq = band[:, 0:FREQS]
        angle, turns, cos_arg, sin_arg, over = (
            squared[:, T * FREQS * i:T * FREQS * (i + 1)]
            .rearrange("p (t f) -> p t f", t=T) for i in range(5))
        ss_mem, rs_mem = stats[:, 0:2], stats[:, 2:4]
        ss_x, rs_x = stats[:, 4:6], stats[:, 6:8]
        ss_ret, rs_ret = stats[:, 8:12], stats[:, 12:16]
        ss_out = stats[:, 16:24].rearrange("p (t b) -> p t b", t=T)
        ss_post, rs_post = stats[:, 24:26], stats[:, 26:28]
        ss_h, rs_h = stats[:, 28:30], stats[:, 30:32]
        top, neg, den, inv = (stats[:, 32 + 4 * i:36 + 4 * i].rearrange("p (a b) -> p a b", a=2) for i in range(4))
        swa_top, swa_neg, swa_den, swa_es, swa_inv = (
            [stats[:, 48 + 8 * i + 4 * r:52 + 8 * i + 4 * r].rearrange("p (e b) -> p e b", e=2) for r in range(2)]
            for i in range(5))
        mean = stats[:, 88:92]
        pos_f = stats[:, 92:94]
        half_rs = [stats[:, 94:96], stats[:, 96:98]]
        rs_layer = (rs_x, rs_h)
        pos_i = sb("pos_i", [P, T], I32)

        acc = ctx.enter_context(nc.psum_tensor("acc", [P, 2, T, N], F32))
        aux = ctx.enter_context(nc.psum_tensor("aux", [P, 4, N], F32))
        turn = [aux[:, i, :] for i in range(2)]
        score = [aux[:, 2 + i, :] for i in range(2)]

        raw_in = [sem(f"raw_in{i}") for i in range(RING)]
        hi_ready, lo_ready = sem("hi_ready"), sem("lo_ready")
        chunk_done = sem("chunk_done")
        acc_drained = [sem("acc_drained0"), sem("acc_drained1")]
        ident_in, freq_in, band_in, gains_in, pos_in, sinks_in = (
            sem(n) for n in ("ident_in", "freq_in", "band_in", "gains_in", "pos_in", "sinks_in"))
        mem_in = [sem(f"mem_in{i}") for i in range(D // PIECE)]
        x_in = sem("x_in")
        post_in, mem_tile_in, decay_in = sem("post_in"), sem("mem_tile_in"), sem("decay_in")
        gains_turned, gains_ready = sem("gains_turned"), sem("gains_ready")
        freq_read, angles_ready, tables_ready = sem("freq_read"), sem("angles_ready"), sem("tables_ready")
        squares = sem("squares")
        consts_ready, means, rsqrt_ready = sem("consts_ready"), sem("means"), sem("rsqrt_ready")
        half_ready = sem("half_ready")
        norm_turned, norm_hi, norm_lo = sem("norm_turned"), sem("norm_hi"), sem("norm_lo")
        tile_turned, tile_hi, tile_lo = sem("tile_turned"), sem("tile_hi"), sem("tile_lo")
        roped = sem("roped")
        block_turned = sem("block_turned")
        block_a, block_b = sem("block_a"), sem("block_b")
        v_hi = sem("v_hi")
        score_full, o_full, o_stored = sem("score_full"), sem("o_full"), sem("o_stored")
        neg_ready, probs_ready, probs_turned = sem("neg_ready"), sem("probs_ready"), sem("probs_turned")
        probs_a, probs_b = sem("probs_a"), sem("probs_b")
        masked_ready = sem("masked_ready")
        tanh_ready, gated_ready, gated_turned = sem("tanh_ready"), sem("gated_ready"), sem("gated_turned")
        mix_hi, mix_lo = sem("mix_hi"), sem("mix_lo")
        out_squares, post_sum = sem("out_squares"), sem("post_sum")
        copies_ready = sem("copies_ready")
        h_ready, final_ready, out_done = sem("h_ready"), sem("final_ready"), sem("out_done")
        dve_step = sem("dve_step")

        R_MEM, R_X, R_RET, R_POST0, R_H, R_POST1 = 1, 2, 3, 7, 8, 9
        B_KV, B_MEM, B_RET, B_SHARED, B_SWA = (0, 12), (2, 15), 4, 14, 17
        ROPE_RET, ROPE_SHARED, ROPE_SWA = 0, 8, 9
        U_MEM, U_RET, U_SWA = (0, 6), 2, 8
        X_MEM, X_SWA = (0, 2), 4
        UNITS = 4

        def drained(eng, b, it=0, per=0):
            eng.wait_ge(acc_drained[b % 2], it * (per // 2) + (b // 2 + 1))

        def unit_slot(p, u):
            return 11 + BLK * p + 2 * u

        def units_at(s, after):
            return [(p, u) for p in range(2) for u in range(UNITS) if unit_slot(p, u) + after == s]

        def natural(a):
            return a[0].rearrange("(t p) n -> p t n", p=P)

        def rows(w):
            return w.rearrange("(k p) n -> p k n", p=P)

        blk = ctx.enter_context(nc.Block())

        @blk.sync
        def _(sp):
            def load(c, slot, w, k, col):
                if not (isinstance(c, int) and c < RING):
                    sp.wait_ge(lo_ready, c - RING + 1)
                sp.dma_start(raw[:, slot], rows(w)[:, k:k + CK, bass.ds(col, N)]).then_inc(raw_in[slot], 16)

            def load_block(c, w, col):
                for i in range(BLK):
                    load(c + i, i % RING, w, CK * i, col)

            def kv(layer, first=0):
                c0 = SECTIONS[f"KV{layer}"][0]
                for b in range(4):
                    for i in range(BLK):
                        if b * BLK + i >= first:
                            load(c0 + b * BLK + i, i % RING, w_mem[layer], CK * i, N * b)
                        if layer == 0 and b == 1 and i % 2 == 0:
                            cols = slice(i // 2 * PIECE, (i // 2 + 1) * PIECE)
                            sp.dma_start(h[:, :, cols], natural(x)[:, :, cols]).then_inc(x_in, 16)

            def memory_blocks(layer, w, col):
                c0 = SECTIONS[f"MEM{layer}"][0]
                for b in range(4):
                    load_block(c0 + BLK * b, w, col + N * b)

            def out_blocks(layer):
                c0 = SECTIONS[f"OUT{layer}"][0]
                with sp.Fori(1, 3) as it:
                    for b in range(2):
                        for i in range(OBLK):
                            g = i // 2
                            k = (KT + 4 * g if g < 2 else 4 * (g - 2)) + CK * (i % 2)
                            load(it * (2 * OBLK) + (c0 + OBLK * (b - 2) + i), i % RING, w_out[layer], k,
                                 it * (2 * N) + N * (b - 2))

            for i in range(D // PIECE):
                cols = slice(i * PIECE, (i + 1) * PIECE)
                sp.dma_start(nat[:, :, cols], natural(mem)[:, :, cols]).then_inc(mem_in[i], 16)
                for c in range(2 * i, min(2 * i + 2, RING)):
                    load(c, c, w_mem[0], CK * c, 0)
            kv(0, first=RING)
            memory_blocks(0, w_in_a[0], 4 * D)
            c0 = SECTIONS["RET"][0]
            with sp.Fori(0, 4) as it:
                for b in range(4):
                    load_block(it * (4 * BLK) + (c0 + BLK * b), w_in_a[0], it * N + D * b)
            out_blocks(0)
            kv(1)
            load_block(SECTIONS["SHARED"][0], w_kv, 0)
            memory_blocks(1, w_in_b[0], 2 * D)
            c0 = SECTIONS["SWA"][0]
            with sp.Fori(0, 2) as it:
                for b in range(4):
                    load_block(it * (4 * BLK) + (c0 + BLK * b), w_in_b[0],
                               it * (2 * N) + (D * (b // 2) + N * (b % 2)))
            out_blocks(1)
            for i in range(D // OUT_PIECE):
                cols = slice(i * OUT_PIECE, (i + 1) * OUT_PIECE)
                sp.wait_ge(final_ready, i + 1)
                sp.dma_start(natural(out)[:, :, cols], nat[:, :, cols]).then_inc(out_done, 16)
            sp.wait_ge(out_done, 16 * (D // OUT_PIECE))

        @blk.gpsimd
        def _(pool):
            pool.dma_start(ident[:, :], c_ident).then_inc(ident_in, 16)
            pool.memset(minus_half[:, :], -0.5)
            pool.memset(ret_eps[:, :], RET_DIM * EPS).then_inc(consts_ready, 1)
            pool.wait_ge(consts_ready, 1)
            pool.dma_start(pos_i[:, :], positions[0].rearrange("(t p) -> p t", p=P),
                           allow_slow_non_contiguous=True).then_inc(pos_in, 16)
            pool.dma_start(freq, c_freq).then_inc(freq_in, 16)
            pool.dma_start(sink_cols[:, :], sinks[0].partition_broadcast(P)).then_inc(sinks_in, 16)

            n_means = Count()

            def rsqrt(total, result, scale, eps):
                width = total.shape[1]
                if not isinstance(n_means.value, int) or n_means.value:
                    pool.wait_ge(rsqrt_ready, n_means.value)
                pool.tensor_scalar(mean[:, 0:width], total, scale, eps, ALU.mult, ALU.add).then_inc(means, 1)
                pool.wait_ge(means, n_means.up())
                pool.tensor_tensor(result, mean[:, 0:width], minus_half[:, 0:width], ALU.pow).then_inc(rsqrt_ready, 1)

            def halve(layer, factors):
                pool.wait_ge(rsqrt_ready, factors)
                pool.tensor_scalar(half_rs[layer], rs_layer[layer], 0.5, None, ALU.mult).then_inc(half_ready, 1)

            pool.wait_ge(squares, 2)
            rsqrt(ss_mem, rs_mem, 1.0 / D, EPS)
            pool.wait_ge(freq_read, 1)
            pool.dma_start(band[:, :], c_band).then_inc(band_in, 16)
            pool.wait_ge(squares, 4)
            rsqrt(ss_x, rs_x, 1.0 / D, EPS)
            halve(0, R_X)
            pool.wait_ge(norm_turned, KT // 2)
            with pool.Fori(0, 4) as it:
                n_means.enter(it, 1)
                pool.dma_start(decay, c_decay[:, bass.ds(it * 2, 2), :]).then_inc(decay_in, 16)
                pool.wait_ge(squares, it * 4 + 8)
                pool.tensor_tensor(mean, ss_ret, ret_eps[:, :], ALU.add).then_inc(means, 1)
                pool.wait_ge(means, n_means.up())
                pool.tensor_tensor(rs_ret, mean, minus_half[:, :], ALU.pow).then_inc(rsqrt_ready, 1)
            n_means.leave(4)
            pool.wait_ge(gated_turned, GROUPS)
            pool.dma_start(post_gain, post_g[0].partition_broadcast(P)).then_inc(post_in, 16)
            for t in range(T):
                if t:
                    pool.wait_ge(tile_turned, 4 * t)
                pool.dma_start(mem_tile, mem[0, t * P:(t + 1) * P, :]).then_inc(mem_tile_in, 16)
            pool.wait_ge(post_sum, 1)
            rsqrt(ss_post, rs_post, 1.0 / D, EPS)
            pool.wait_ge(squares, 22)
            rsqrt(ss_h, rs_h, 1.0 / D, EPS)
            halve(1, R_H)
            pool.wait_ge(block_a, B_SHARED + 1)
            pool.wait_ge(block_b, B_SHARED + 1)
            with pool.Fori(0, 2) as it:
                pool.wait_ge(o_full, it * (2 * UNITS) + U_SWA)
                pool.tensor_copy(swa_kt, shared_kt[:, bass.ds(it * 2, 2), :])
                pool.tensor_copy(swa_v, shared_v[:, :, bass.ds(it * (2 * SWA_DIM), 2 * SWA_DIM)]).then_inc(copies_ready, 1)
            pool.wait_ge(gated_turned, 2 * GROUPS)
            pool.dma_start(post_gain, post_g[1].partition_broadcast(P)).then_inc(post_in, 16)
            pool.wait_ge(post_sum, 2)
            rsqrt(ss_post, rs_post, 1.0 / D, EPS)

        @blk.scalar
        def _(act):
            for r0, g in ((0, pre_g), (2 * KT, mem_g)):
                act.dma_start(gain_rows[r0:r0 + 2 * KT, :],
                              g.rearrange("l (k p) -> (l k) p", p=P)).then_inc(gains_in, 16)
            act.dma_start(gain_rows[4 * KT:GAINS, :], kv_g.rearrange("(k p) -> k p", p=P)).then_inc(gains_in, 16)

            def copy(dst, src, **kw):
                return nc.scalar.activation(dst, src, ACT.Copy, **kw)

            def split(c, slot):
                if isinstance(c, int) and c >= CHUNKS:
                    return
                act.wait_ge(raw_in[slot], c * (16 // RING) + (16 - slot * (16 // RING)))
                if not (isinstance(c, int) and c < RING):
                    act.wait_ge(chunk_done, c - RING + 1)
                copy(weight_hi[:, slot], raw[:, slot]).then_inc(hi_ready, 1)

            def sum_squares(src, total, scratch):
                return nc.scalar.activation(scratch, src, ACT.Square, accum_out=total)

            def norm_part(g, dst, gain):
                act.wait_ge(norm_turned, g + 1)
                i = g % (KT // 2)
                for j in range(2):
                    last = copy(dst[:, 2 * i + j, :], aux[:, g % 4, S * j:S * (j + 1)],
                                scale=gains[:, gain + 2 * i + j:gain + 2 * i + j + 1])
                last.then_inc(norm_hi, 1)

            def copy_block(c_end, par, rs):
                act.wait_ge(chunk_done, c_end)
                for t in range(T):
                    last = copy(block[:, t, :], acc[:, par, t, :], scale=rs[:, t:t + 1])
                last.then_inc(acc_drained[par], 1)

            def store_half(n, dst):
                act.wait_ge(block_turned, n + 1)
                copy(dst, turn[0]).then_inc(block_a, 1)

            def store_hi(n, dst):
                act.wait_ge(block_turned, n + 1)
                for i in range(2):
                    last = copy(dst[:, 2 * i:2 * i + 2, :], turn[i])
                last.then_inc(block_a, 1)

            def mix_part(g, pos):
                act.wait_ge(gated_turned, g + 1)
                for i in range(2):
                    copy(b_hi[:, bass.ds(pos * 4 + 2 * i, 2), :], turn[i]).then_inc(mix_hi, 1)

            def tanh_gate(layer, g, c_end, par):
                act.wait_ge(chunk_done, c_end)
                if not (isinstance(g, int) and g == 0):
                    act.wait_ge(gated_ready, g)
                for t in range(T):
                    nc.scalar.activation(gate[:, t, :], acc[:, par, t, :], ACT.Tanh,
                                         scale=half_rs[layer][:, t:t + 1]).then_inc(tanh_ready, 1)

            for c in range(AHEAD):
                split(c, c)
                if c == 0:
                    act.wait_ge(gains_ready, 1)
                norm_part(c, b_hi, 2 * KT)

            def kv(layer):
                c0, b0 = SECTIONS[f"KV{layer}"]
                for s in range(4 * BLK):
                    split(c0 + s + AHEAD, (s + AHEAD) % RING)
                    if layer == 0 and s + AHEAD < KT // 2:
                        norm_part(s + AHEAD, b_hi, 2 * KT)
                    for i, (src, total) in enumerate(((nat, ss_mem), (h, ss_x))):
                        if layer == 0 and s in (5 + 23 * i, 6 + 23 * i):
                            t = s - 5 - 23 * i
                            if t:
                                act.wait_ge(squares, T * i + t)
                            sum_squares(src[:, t, :], total[:, t:t + 1], squared).then_inc(squares, 1)
                    if layer == 0 and s == 19:
                        act.wait_ge(angles_ready, 2)
                        for arg, ret, swa in ((cos_arg, ret_cos, swa_cos), (sin_arg, ret_sin, swa_sin)):
                            nc.scalar.activation(ret, arg[:, :, 0:HALF], ACT.Sin)
                            last = nc.scalar.activation(swa, arg[:, :, HALF:FREQS], ACT.Sin)
                        last.then_inc(tables_ready, 1)
                    if layer == 1 and s in (2, 3):
                        t = s - 2
                        act.wait_ge(h_ready, t + 1)
                        sum_squares(h[:, t, :], ss_h[:, t:t + 1], nat[:, t, :]).then_inc(squares, 1)
                    if 20 <= s < 20 + KT // 2:
                        norm_part((layer + 1) * KT // 2 + s - 20, (a_hi, b_hi)[layer], (0, 4 * KT)[layer])
                    for p in range(2):
                        if s == BLK * (p + 1):
                            n = B_KV[layer] + p
                            if n:
                                act.wait_ge(block_turned, n)
                            if layer == 0:
                                act.wait_ge(rsqrt_ready, R_MEM)
                            elif p == 0:
                                act.wait_ge(post_sum, 1)
                            copy_block(c0 + s, (b0 + p) % 2, rs_mem)
                        if s == BLK * (p + 1) + 2:
                            store_hi(B_KV[layer] + p, mem_kt[:, 4 * p:4 * p + 4, :])
                    if s == 3 * BLK:
                        store_v(c0 + s, b0 + 2, 0)
                return lambda: store_v(c0 + 4 * BLK, b0 + 3, 1)

            def store_v(c_end, b, i):
                act.wait_ge(chunk_done, c_end)
                for t in range(T):
                    last = copy(mem_v[:, t, N * i:N * (i + 1)], acc[:, b % 2, t, :], scale=rs_mem[:, t:t + 1])
                last.then_inc(v_hi, 1)

            def memory(layer):
                c0, b0 = SECTIONS[f"MEM{layer}"]
                for s in range(4 * BLK):
                    split(c0 + s + AHEAD, (s + AHEAD) % RING)
                    if s == 0:
                        act.wait_ge(rsqrt_ready, (R_X, R_H)[layer])
                    if layer == 1 and s == 0:
                        act.wait_ge(chunk_done, c0)
                        act.wait_ge(block_turned, B_SHARED)
                        par = (b0 - 1) % 2
                        kw = KV_HEADS * SWA_DIM
                        for t in range(T):
                            k = acc[:, par, t, 0:kw].rearrange("p (h a d) -> p h a d", h=KV_HEADS, a=1)
                            for dup in range(2):
                                copy(block[:, t, :].rearrange("p (h a d) -> p h a d", h=KV_HEADS, a=2)[:, :, dup:dup + 1, :],
                                     k, scale=rs_h[:, t:t + 1])
                            last = copy(shared_v[:, t, :], acc[:, par, t, kw:2 * kw], scale=rs_h[:, t:t + 1])
                        last.then_inc(acc_drained[par], 1)
                    if layer == 1 and s == 4:
                        store_half(B_SHARED, shared_kt[:, 0:2, :])
                    for p in range(2):
                        n, u, x = B_MEM[layer] + p, U_MEM[layer] + p, X_MEM[layer] + p
                        if s == 8 + BLK * p:
                            act.wait_ge(block_turned, n)
                            copy_block(c0 + s, (b0 + p) % 2, rs_layer[layer])
                        if s == 10 + BLK * p:
                            if p:
                                act.wait_ge(score_full, u)
                            store_hi(n, mem_q_hi)
                        if s == 12 + BLK * p:
                            act.wait_ge(neg_ready, x + 1)
                            if x:
                                act.wait_ge(probs_turned, x)
                            for t in range(T):
                                for j in range(2):
                                    last = nc.scalar.activation(
                                        mem_p[:, t, j, :], score[t][:, S * j:S * (j + 1)], ACT.Exp,
                                        bias=neg[:, t, j:j + 1], scale=RET_DIM ** -0.5, accum_out=den[:, t, j:j + 1])
                            last.then_inc(probs_ready, 1)
                        if s == 15 + BLK * p:
                            act.wait_ge(probs_turned, x + 1)
                            if p:
                                act.wait_ge(o_full, u)
                            for j in range(2):
                                last = copy(mem_pt_hi[:, 2 * j:2 * j + 2, :], turn[j])
                            last.then_inc(probs_a, 1)
                    if s == 24:
                        act.wait_ge(half_ready, layer + 1)
                        tanh_gate(layer, GROUPS * layer, c0 + s, b0 % 2)
                    if s == 27:
                        mix_part(GROUPS * layer, 0)
                tanh_gate(layer, GROUPS * layer + 1, c0 + 4 * BLK, (b0 + 1) % 2)

            finish_v = kv(0)
            finish_v()
            memory(0)

            c0, b0 = SECTIONS["RET"]
            with act.Fori(0, 4) as it:
                for s in range(4 * BLK):
                    split(it * (4 * BLK) + (c0 + s + AHEAD), (s + AHEAD) % RING)
                    if s == 3:
                        mix_part(it + 1, it + 1)
                    if s == 12:
                        act.wait_ge(score_full, it + U_RET)
                        store_hi(it * 2 + B_RET, ret_q_hi)
                    if s == 20:
                        store_hi(it * 2 + (B_RET + 1), ret_k_hi)
                    if s == 24:
                        act.wait_ge(chunk_done, it * (4 * BLK) + (c0 + s))
                        act.wait_ge(o_full, it + U_RET)
                        for t in range(T):
                            last = copy(v_nat[:, t, :], acc[:, (b0 + 2) % 2, t, :], scale=rs_x[:, t:t + 1])
                        last.then_inc(acc_drained[(b0 + 2) % 2], 1)
                    if s == 26:
                        act.wait_ge(o_full, it + (U_RET + 1))
                        act.wait_ge(gated_ready, it + 2)
                        for t in range(T):
                            for j in range(2):
                                sum_squares(score[t][:, RET_DIM * j:RET_DIM * (j + 1)], ss_ret[:, 2 * t + j:2 * t + j + 1],
                                            junk[:, (2 * t + j) * RET_DIM:(2 * t + j + 1) * RET_DIM]).then_inc(squares, 1)
                act.wait_ge(squares, it * 4 + 8)
                tanh_gate(0, it + 2, it * (4 * BLK) + (c0 + 4 * BLK), (b0 + 3) % 2)

            def out_pass(layer, it):
                c0, b0 = SECTIONS[f"OUT{layer}"]
                for b in range(2):
                    for i in range(OBLK):
                        s = OBLK * b + i
                        split(it * (2 * OBLK) + (c0 + s + AHEAD), (s + AHEAD) % RING)
                        if it == 0 and s == 3:
                            mix_part(GROUPS * (layer + 1) - 1, GROUPS - 1)
                        if s == OBLK:
                            out_part(layer, it, 0, c0, b0)
                        if layer == 0 and s in (8, 11, 14, 17):
                            g = (s - 8) // 3
                            act.wait_ge(tile_turned, it * 4 + (g + 1))
                            for j in range(4):
                                k = 4 * g + j
                                last = copy(a_hi[:, k, bass.ds(it * P, P)], aux[:, g, P * j:P * (j + 1)],
                                            scale=gains[:, 3 * KT + k:3 * KT + k + 1])
                            last.then_inc(tile_hi, 1)
                out_part(layer, it, 1, c0, b0)

            def out_part(layer, it, b, c0, b0):
                act.wait_ge(chunk_done, it * (2 * OBLK) + (c0 + OBLK * (b + 1)))
                if not (isinstance(it, int) and it + b + layer == 0):
                    act.wait_ge(out_squares, it * 4 + (8 * layer + 2 * b))
                for t in range(T):
                    sum_squares(acc[:, (b0 + b) % 2, t, :], ss_out[:, t, bass.ds(it * 2 + b, 1)],
                                junk[:, N * t:N * (t + 1)]).then_inc(out_squares, 1)

            for it in range(2):
                out_pass(0, it)
            finish_v = kv(1)
            for s in range(BLK):
                split(SECTIONS["SHARED"][0] + s + AHEAD, (s + AHEAD) % RING)
                if s == 0:
                    finish_v()
                norm_part(3 * KT // 2 + s, a_hi, KT)
            memory(1)

            c0, b0 = SECTIONS["SWA"]
            with act.Fori(0, 2) as it:
                c_it = it * (4 * BLK)
                for s in range(4 * BLK):
                    if s == 3:
                        mix_part(it * 2 + (GROUPS + 1), it * 2 + 1)
                    for p in range(2):
                        if s == 8 + BLK * p:
                            act.wait_ge(block_turned, it * 2 + (B_SWA + p))
                            copy_block(c_it + (c0 + s), (b0 + p) % 2, rs_h)
                        if s == 10 + BLK * p:
                            act.wait_ge(score_full, it * (2 * UNITS) + (U_SWA + UNITS * p))
                            store_half(it * 2 + (B_SWA + p), q_t[:, 0:2, :])
                    for p, u in units_at(s, 1):
                        x = it * (2 * UNITS) + (X_SWA + UNITS * p + u)
                        r = u % 2
                        act.wait_ge(neg_ready, x + 1)
                        for e in range(2):
                            for j, (lo, hi) in enumerate(((0, P), (P, 3 * P))):
                                nc.scalar.activation(swa_p[:, r, e, lo:hi], swa_p[:, r, e, lo:hi], ACT.Exp,
                                                     bias=swa_neg[r][:, e, j:j + 1], scale=SWA_DIM ** -0.5,
                                                     accum_out=swa_den[r][:, e, j:j + 1])
                            last = nc.scalar.activation(swa_es[r][:, e, :], swa_neg[r][:, e, :], ACT.Exp,
                                                        bias=sink_cols[:, bass.ds(it * 16 + (8 * p + 2 * u + e), 1)])
                        last.then_inc(probs_ready, 1)
                    for p, u in units_at(s, 4):
                        x = it * (2 * UNITS) + (X_SWA + UNITS * p + u)
                        act.wait_ge(probs_turned, x + 1)
                        act.wait_ge(o_full, it * (2 * UNITS) + (U_SWA + UNITS * p + u - 1))
                        copy(swa_pt[:, u % 2, 0, :], turn[0][:, 0:3 * P]).then_inc(probs_a, 1)
                    if s == 24:
                        tanh_gate(1, it * 2 + (GROUPS + 2), c_it + (c0 + s), b0 % 2)
                    if s == 28:
                        mix_part(it * 2 + (GROUPS + 2), it * 2 + 2)
                    split(c_it + (c0 + s + AHEAD), (s + AHEAD) % RING)
                tanh_gate(1, it * 2 + (GROUPS + 3), c_it + (c0 + 4 * BLK), (b0 + 1) % 2)

            for it in range(2):
                out_pass(1, it)

        @blk.vector
        def _(dve):
            n_steps = Count()

            def step(ins):
                ins.then_inc(dve_step, 1)
                dve.wait_ge(dve_step, n_steps.up())

            def split(c, slot):
                if isinstance(c, int) and c >= CHUNKS:
                    return
                dve.wait_ge(hi_ready, c + 1)
                dve.tensor_tensor(weight_lo[:, slot], raw[:, slot], weight_hi[:, slot].bitcast(F32),
                                  ALU.subtract).then_inc(lo_ready, 1)

            def norm_part(g, dst_hi, dst_lo, gain):
                dve.wait_ge(norm_hi, g + 1)
                i = g % (KT // 2)
                for j in range(2):
                    k = 2 * i + j
                    last = dve.scalar_tensor_tensor(dst_lo[:, k, :], aux[:, g % 4, S * j:S * (j + 1)],
                                                    gains[:, gain + k:gain + k + 1],
                                                    dst_hi[:, k, :].bitcast(F32), ALU.mult, ALU.subtract)
                last.then_inc(norm_lo, 1)

            def store_half(n, dst):
                dve.wait_ge(block_turned, n + 1)
                dve.tensor_copy(dst, turn[1]).then_inc(block_b, 1)

            def store_lo(n, hi, lo):
                dve.wait_ge(block_a, n + 1)
                for i in range(2):
                    at = slice(2 * i, 2 * i + 2)
                    last = dve.tensor_tensor(lo[:, at, :], turn[i], hi[:, at, :].bitcast(F32), ALU.subtract)
                last.then_inc(block_b, 1)

            def store_v_lo(n, i, b):
                dve.wait_ge(v_hi, n + 1)
                cols = slice(N * i, N * (i + 1))
                for t in range(T):
                    last = dve.scalar_tensor_tensor(mem_v_lo[:, t, cols], acc[:, b % 2, t, :], rs_mem[:, t:t + 1],
                                                    mem_v[:, t, cols].bitcast(F32), ALU.mult, ALU.subtract)
                last.then_inc(acc_drained[b % 2], 1)

            def mix_part(g, pos):
                dve.wait_ge(mix_hi, g * 2 + 2)
                for i in range(2):
                    at = bass.ds(pos * 4 + 2 * i, 2)
                    last = dve.tensor_tensor(b_lo[:, at, :], turn[i], b_hi[:, at, :].bitcast(F32), ALU.subtract)
                last.then_inc(mix_lo, 1)

            def gate_group(layer, g, dst, par, drains):
                for t in range(T):
                    dve.wait_ge(tanh_ready, g * 2 + (t + 1))
                    last = dve.scalar_tensor_tensor(gate[:, t, :], gate[:, t, :], 1.0, acc[:, par, t, :],
                                                    ALU.add, ALU.mult)
                last.then_inc(acc_drained[par], 1)
                dve.wait_ge(acc_drained[par], drains)
                for t in range(T):
                    last = dve.scalar_tensor_tensor(dst[:, t, :], dst[:, t, :], rs_layer[layer][:, t:t + 1],
                                                    gate[:, t, :], ALU.mult, ALU.mult)
                last.then_inc(gated_ready, 1)

            def rope_window(n):
                for t in range(T):
                    v = block[:, t, :].rearrange("p (h d) -> p h d", d=SWA_DIM)
                    x1, x2 = v[:, :, 0:RH], v[:, :, RH:ROT]
                    heads = N // SWA_DIM
                    cos, sin = (f[:, t, :].unsqueeze(1).to_broadcast([P, heads, RH]) for f in (swa_cos, swa_sin))
                    xs = [(rope_a, rope_b)[t][:, heads * RH * i:heads * RH * (i + 1)].rearrange("p (h d) -> p h d", h=heads) for i in range(4)]
                    dve.tensor_tensor(xs[0], x1, cos, ALU.mult)
                    dve.tensor_tensor(xs[1], x2, sin, ALU.mult)
                    dve.tensor_tensor(xs[2], x2, cos, ALU.mult)
                    step(dve.tensor_tensor(xs[3], x1, sin, ALU.mult))
                    dve.tensor_tensor(x1, xs[0], xs[1], ALU.subtract)
                    last = dve.tensor_tensor(x2, xs[2], xs[3], ALU.add)
                last.then_inc(roped, 1)

            def angles():
                dve.wait_ge(pos_in, 16)
                dve.wait_ge(freq_in, 16)
                step(dve.tensor_copy(pos_f, pos_i[:, :]))
                for t in range(T):
                    last = dve.tensor_scalar(angle[:, t, :], freq, pos_f[:, t:t + 1], None, ALU.mult)
                last.then_inc(freq_read, 1)
                dve.wait_ge(freq_read, 1)

            def reduced(arg, quarter):
                step(dve.tensor_scalar(turns, angle, 1.0 / TWO_PI, quarter, ALU.mult, ALU.add))
                step(dve.tensor_scalar(turns, turns, ROUND, -ROUND, ALU.add, ALU.add))
                step(dve.scalar_tensor_tensor(arg, turns, -TWO_PI_1, angle, ALU.mult, ALU.add))
                step(dve.scalar_tensor_tensor(arg, turns, -TWO_PI_2, arg, ALU.mult, ALU.add))
                step(dve.scalar_tensor_tensor(arg, turns, -TWO_PI_3, arg, ALU.mult, ALU.add))
                step(dve.tensor_scalar(arg, arg, quarter * TWO_PI, None, ALU.add))
                step(dve.tensor_scalar(over, arg, PI, -TWO_PI, ALU.is_gt, ALU.mult))
                step(dve.tensor_tensor(arg, arg, over, ALU.add))
                step(dve.tensor_scalar(over, arg, -PI, TWO_PI, ALU.is_lt, ALU.mult))
                step(dve.tensor_tensor(arg, arg, over, ALU.add))
                dve.tensor_scalar(arg, arg, PI_DOWN, -PI_DOWN, ALU.min, ALU.max).then_inc(angles_ready, 1)

            dve.wait_ge(gains_turned, 1)
            dve.tensor_copy(gains[:, :], aux[:, 3, 0:GAINS]).then_inc(gains_ready, 1)
            for c in range(AHEAD):
                if c < LO_AHEAD:
                    split(c, c)
                norm_part(c, b_hi, b_lo, 2 * KT)

            def kv(layer):
                c0, b0 = SECTIONS[f"KV{layer}"]
                for s in range(4 * BLK):
                    split(c0 + s + LO_AHEAD, (s + LO_AHEAD) % RING)
                    if layer == 0 and s + AHEAD < KT // 2:
                        norm_part(s + AHEAD, b_hi, b_lo, 2 * KT)
                    if layer == 0 and s == 11:
                        angles()
                        reduced(cos_arg, 0.25)
                    if layer == 0 and s == 14:
                        reduced(sin_arg, 0.0)
                        dve.wait_ge(sinks_in, 16)
                        dve.tensor_scalar(neg_sinks[:, :], sink_cols[:, :], -1.0, None, ALU.mult)
                    if layer == 1 and s == 0:
                        post_total(0)
                    if layer == 1 and s in (1, 2):
                        t = s - 1
                        dve.wait_ge(rsqrt_ready, R_POST0)
                        dve.scalar_tensor_tensor(h[:, t, :], nat[:, t, :], rs_post[:, t:t + 1], h[:, t, :],
                                                 ALU.mult, ALU.add).then_inc(h_ready, 1)
                    if 20 <= s < 20 + KT // 2:
                        norm_part((layer + 1) * KT // 2 + s - 20, (a_hi, b_hi)[layer], (a_lo, b_lo)[layer],
                                  (0, 4 * KT)[layer])
                    for p in range(2):
                        if s == BLK * (p + 1) + 2:
                            at = slice(4 * p, 4 * p + 4)
                            store_lo(B_KV[layer] + p, mem_kt[:, at, :], mem_kt_lo[:, at, :])
                    if s == 3 * BLK:
                        store_v_lo(2 * layer, 0, b0 + 2)

            def memory(layer):
                c0, b0 = SECTIONS[f"MEM{layer}"]
                for s in range(4 * BLK):
                    split(c0 + s + LO_AHEAD, (s + LO_AHEAD) % RING)
                    if s == 5:
                        dve.wait_ge(rsqrt_ready, (R_X, R_H)[layer])
                    if layer == 0 and s == 5:
                        dve.wait_ge(tables_ready, 1)
                        for t in range(T):
                            for table in (ret_cos, ret_sin):
                                last = dve.tensor_scalar(table[:, t, :], table[:, t, :], rs_x[:, t:t + 1], None, ALU.mult)
                        step(last)
                    if layer == 1 and s == 1:
                        drained(dve, b0 - 1)
                        rope_window(ROPE_SHARED)
                    if layer == 1 and s == 4:
                        store_half(B_SHARED, shared_kt[:, 2:4, :])
                    for p in range(2):
                        n, u, x = B_MEM[layer] + p, U_MEM[layer] + p, X_MEM[layer] + p
                        if s == 10 + BLK * p:
                            store_lo(n, mem_q_hi, mem_q_lo)
                        if s == 12 + BLK * p:
                            dve.wait_ge(score_full, u + 1)
                            for t in range(T):
                                last = dve.tensor_reduce(top[:, t, :], score[t].rearrange("p (h m) -> p h m", h=2),
                                                         AX.X, ALU.max)
                            step(last)
                            dve.tensor_scalar(neg, top, -RET_DIM ** -0.5, None, ALU.mult).then_inc(neg_ready, 1)
                        if s == 15 + BLK * p:
                            dve.wait_ge(probs_a, x + 1)
                            dve.reciprocal(inv, den)
                            for j in range(2):
                                at = slice(2 * j, 2 * j + 2)
                                last = dve.tensor_tensor(mem_pt_lo[:, at, :], turn[j], mem_pt_hi[:, at, :].bitcast(F32),
                                                         ALU.subtract)
                            last.then_inc(probs_b, 1)
                            dve.wait_ge(probs_b, x + 1)
                        if s == 17 + BLK * p:
                            dve.wait_ge(o_full, u + 1)
                            store_o(p, [inv[:, t, :] for t in range(T)])
                    if s == 25:
                        gate_group(layer, GROUPS * layer, gated[0], b0 % 2, (b0 + 2) // 2 + 1)
                    if s == 27:
                        mix_part(GROUPS * layer, 0)
                gate_group(layer, GROUPS * layer + 1, gated[1], (b0 + 1) % 2, (b0 + 3) // 2 + 1)

            def store_o(i, factors, scale=0.5):
                for t in range(T):
                    o = score[t].rearrange("p (h d) -> p h d", h=2)
                    last = dve.scalar_tensor_tensor(gated[i][:, t, :].rearrange("p (h d) -> p h d", h=2), o, scale,
                                                    factors[t].unsqueeze(2).to_broadcast([P, 2, RET_DIM]),
                                                    ALU.mult, ALU.mult)
                last.then_inc(o_stored, 1)

            def post_total(layer):
                dve.wait_ge(out_squares, 8 * (layer + 1))
                dve.tensor_reduce(ss_post, ss_out, AX.X, ALU.add).then_inc(post_sum, 1)

            kv(0)
            store_v_lo(1, 1, SECTIONS["KV0"][1] + 3)
            memory(0)

            c0, b0 = SECTIONS["RET"]
            with dve.Fori(0, 4) as it:
                n_steps.enter(it, 4)
                for s in range(4 * BLK):
                    split(it * (4 * BLK) + (c0 + s + LO_AHEAD), (s + LO_AHEAD) % RING)
                    if s == 3:
                        mix_part(it + 1, it + 1)
                    for j in range(2):
                        if s == 8 + BLK * j:
                            par = (b0 + j) % 2
                            dve.wait_ge(chunk_done, it * (4 * BLK) + (c0 + s))
                            dve.wait_ge(block_turned, it * 2 + (B_RET + j))
                            for t in range(T):
                                z = acc[:, par, t, :].rearrange("p (a f) -> p a f", f=HALF)
                                zh = acc[:, par, t, :].rearrange("p (h a f) -> p h a f", h=2, a=2)
                                ra = rope_a.rearrange("p (a f) -> p a f", f=HALF)
                                ah, bh, oh = (v.rearrange("p (h a f) -> p h a f", h=2, a=2)
                                              for v in (rope_a, rope_b, block[:, t, :]))
                                cos = ret_cos[:, t, :].unsqueeze(1).to_broadcast([P, 4, HALF])
                                sin = ret_sin[:, t, :].unsqueeze(1).to_broadcast([P, 2, HALF])
                                dve.tensor_tensor(ra, z, cos, ALU.mult)
                                dve.tensor_tensor(bh[:, :, 0, :], zh[:, :, 1, :], sin, ALU.mult)
                                last = dve.tensor_tensor(bh[:, :, 1, :], zh[:, :, 0, :], sin, ALU.mult)
                                if t == 0:
                                    step(last)
                                else:
                                    last.then_inc(acc_drained[par], 1)
                                    drained(dve, b0 + j, it, 4)
                                dve.tensor_tensor(oh[:, :, 0, :], ah[:, :, 0, :], bh[:, :, 0, :], ALU.subtract)
                                last = dve.tensor_tensor(oh[:, :, 1, :], ah[:, :, 1, :], bh[:, :, 1, :], ALU.add)
                                if t == 0:
                                    step(last)
                            last.then_inc(roped, 1)
                    if s == 12:
                        store_lo(it * 2 + B_RET, ret_q_hi, ret_q_lo)
                    if s == 20:
                        store_lo(it * 2 + (B_RET + 1), ret_k_hi, ret_k_lo)
                    if s == 23:
                        dve.wait_ge(score_full, it + (U_RET + 1))
                        dve.wait_ge(decay_in, it * 16 + 16)
                        dve.wait_ge(o_full, it + U_RET)
                        for j in range(2):
                            last = dve.tensor_tensor(masked[:, j, :], score[j][:, 0:3 * P], decay[:, j, :], ALU.mult)
                        last.then_inc(masked_ready, 1)
                    if s == 27:
                        dve.wait_ge(rsqrt_ready, it + R_RET)
                        dve.wait_ge(gated_turned, it + 2)
                        store_o(1, [rs_ret[:, 2 * t:2 * t + 2] for t in range(T)], RET_DIM ** 0.5 / 2)
                gate_group(0, it + 2, gated[1], (b0 + 3) % 2, it * 2 + ((b0 + 3) // 2 + 1))
            n_steps.leave(4)

            def out_pass(layer, it):
                c0, b0 = SECTIONS[f"OUT{layer}"]
                for b in range(2):
                    for i in range(OBLK):
                        s = OBLK * b + i
                        split(it * (2 * OBLK) + (c0 + s + LO_AHEAD), (s + LO_AHEAD) % RING)
                        if it == 0 and s == 3:
                            mix_part(GROUPS * (layer + 1) - 1, GROUPS - 1)
                        if s == OBLK:
                            out_part(layer, it, 0, b0)
                        if layer == 0 and s in (8, 11, 14, 17):
                            g = (s - 8) // 3
                            dve.wait_ge(tile_hi, it * 4 + (g + 1))
                            for j in range(4):
                                k = 4 * g + j
                                at = bass.ds(it * P, P)
                                last = dve.scalar_tensor_tensor(a_lo[:, k, at], aux[:, g, P * j:P * (j + 1)],
                                                                gains[:, 3 * KT + k:3 * KT + k + 1],
                                                                a_hi[:, k, at].bitcast(F32), ALU.mult, ALU.subtract)
                            last.then_inc(tile_lo, 1)
                out_part(layer, it, 1, b0)

            def out_part(layer, it, b, b0):
                par = (b0 + b) % 2
                dve.wait_ge(out_squares, it * 4 + (8 * layer + 2 * b + 2))
                dve.wait_ge(post_in, 16 * (layer + 1))
                if layer == 1 and it == b == 1:
                    post_total(1)
                at = bass.ds(it * (2 * N) + N * b, N)
                for t in range(T):
                    last = dve.tensor_tensor(nat[:, t, at], acc[:, par, t, :], post_gain[:, at], ALU.mult)
                last.then_inc(acc_drained[par], 1)

            for it in range(2):
                out_pass(0, it)
            drained(dve, SECTIONS["OUT0"][1] + 2)
            drained(dve, SECTIONS["OUT0"][1] + 3)
            kv(1)
            for s in range(BLK):
                split(SECTIONS["SHARED"][0] + s + LO_AHEAD, (s + LO_AHEAD) % RING)
                if s == 0:
                    store_v_lo(3, 1, SECTIONS["KV1"][1] + 3)
                norm_part(3 * KT // 2 + s, a_hi, a_lo, KT)
            memory(1)

            dve.wait_ge(band_in, 16)
            c0, b0 = SECTIONS["SWA"]
            with dve.Fori(0, 2) as it:
                n_steps.enter(it, 2 * (T + 4 * UNITS))
                for s in range(4 * BLK):
                    if s == 3:
                        mix_part(it * 2 + (GROUPS + 1), it * 2 + 1)
                    for p, u in units_at(s, 1):
                        un = it * (2 * UNITS) + (U_SWA + UNITS * p + u)
                        x = it * (2 * UNITS) + (X_SWA + UNITS * p + u)
                        r = u % 2
                        dve.wait_ge(score_full, un + 1)
                        dve.wait_ge(probs_turned, x - 1)
                        dve.tensor_tensor(swa_p[:, r, 0, 0:P], score[0][:, 0:P], band[:, 0:P], ALU.add)
                        for e, j, lo, hi in ((0, 1, P, 3 * P), (1, 0, 0, P), (1, 1, P, 3 * P)):
                            last = dve.tensor_tensor_reduce(
                                swa_p[:, r, e, lo:hi], score[e][:, lo:hi], band[:, lo:hi], 1.0, -3e38,
                                ALU.add, ALU.max, swa_top[r][:, e, j:j + 1])
                        step(last)
                        step(dve.tensor_reduce(swa_top[r][:, 0, 0:1], swa_p[:, r, 0, 0:P], AX.X, ALU.max))
                        for e in range(2):
                            last = dve.tensor_scalar(swa_neg[r][:, e, :], swa_top[r][:, e, :], -SWA_DIM ** -0.5,
                                                     neg_sinks[:, bass.ds(it * 16 + (8 * p + 2 * u + e), 1)],
                                                     ALU.mult, ALU.min)
                        last.then_inc(neg_ready, 1)
                    for p, u in units_at(s, 6):
                        un = it * (2 * UNITS) + (U_SWA + UNITS * p + u)
                        dve.wait_ge(o_full, un + 1)
                        dve.wait_ge(gated_turned, it * 2 + (GROUPS + 1 + p))
                        for e in range(2):
                            col = (2 * u + e) * SWA_DIM
                            last = dve.scalar_tensor_tensor(
                                gated[p][:, :, col:col + SWA_DIM],
                                score[e][:, 3 * P:N].rearrange("p (t d) -> p t d", t=T), 0.5,
                                swa_inv[u % 2][:, e, :].unsqueeze(2).to_broadcast([P, T, SWA_DIM]),
                                ALU.mult, ALU.mult)
                        last.then_inc(o_stored, 1)
                    for p, u in units_at(s, 2):
                        r = u % 2
                        dve.wait_ge(probs_ready, it * (2 * UNITS) + (X_SWA + UNITS * p + u + 1))
                        dve.wait_ge(o_stored, it * (2 * UNITS) + (U_SWA + UNITS * p + u - 1))
                        step(dve.tensor_tensor(swa_den[r], swa_den[r], swa_es[r], ALU.add))
                        step(dve.reciprocal(swa_inv[r], swa_den[r]))
                    for p, u in units_at(s, 4):
                        x = it * (2 * UNITS) + (X_SWA + UNITS * p + u)
                        dve.wait_ge(probs_turned, x + 1)
                        dve.wait_ge(o_full, it * (2 * UNITS) + (U_SWA + UNITS * p + u - 1))
                        dve.tensor_copy(swa_pt[:, u % 2, 1, :], turn[1][:, 0:3 * P]).then_inc(probs_b, 1)
                    for p in range(2):
                        if s == 8 + BLK * p:
                            drained(dve, b0 + p, it, 4)
                            rope_window(it * 2 + (ROPE_SWA + p))
                        if s == 10 + BLK * p:
                            dve.wait_ge(score_full, it * (2 * UNITS) + (U_SWA + UNITS * p))
                            store_half(it * 2 + (B_SWA + p), q_t[:, 2:4, :])
                    if s == 25:
                        dve.wait_ge(o_stored, it * (2 * UNITS) + (U_SWA + UNITS))
                        gate_group(1, it * 2 + (GROUPS + 2), gated[0], b0 % 2, it * 2 + ((b0 + 2) // 2 + 1))
                    if s == 28:
                        mix_part(it * 2 + (GROUPS + 2), it * 2 + 2)
                    split(it * (4 * BLK) + (c0 + s + LO_AHEAD), (s + LO_AHEAD) % RING)
                dve.wait_ge(o_stored, it * (2 * UNITS) + (U_SWA + 2 * UNITS))
                gate_group(1, it * 2 + (GROUPS + 3), gated[1], (b0 + 1) % 2, it * 2 + ((b0 + 3) // 2 + 1))
            n_steps.leave(2)

            for it in range(2):
                out_pass(1, it)
            drained(dve, SECTIONS["OUT1"][1] + 2)
            drained(dve, SECTIONS["OUT1"][1] + 3)
            dve.wait_ge(rsqrt_ready, R_POST1)
            for i in range(D // OUT_PIECE):
                cols = slice(i * OUT_PIECE, (i + 1) * OUT_PIECE)
                for t in range(T):
                    last = dve.scalar_tensor_tensor(nat[:, t, cols], nat[:, t, cols], rs_post[:, t:t + 1],
                                                    h[:, t, cols], ALU.mult, ALU.add)
                last.then_inc(final_ready, 1)

        @blk.tensor
        def _(pe):
            def chunk(c, slot, par, i, blocks, hi, lo):
                pe.wait_ge(lo_ready, c + 1)
                for j in range(CK):
                    k = CK * i + j
                    for t in range(T):
                        tok = slice(t * P, (t + 1) * P)
                        first, last = i == 0 and j == 0, i == blocks - 1 and j == CK - 1
                        o = acc[:, par, t, :]
                        mm = three_passes(o, hi[:, k, tok], lo[:, k, tok], weight_hi[:, slot, j, :],
                                          weight_lo[:, slot, j, :], first, last)
                mm.then_inc(chunk_done, 1)

            def three_passes(o, st_hi, st_lo, mv_hi, mv_lo, first, last):
                pe.matmul(o, st_hi, mv_hi, start=first, stop=False)
                pe.matmul(o, st_hi, mv_lo, start=False, stop=False)
                return pe.matmul(o, st_lo, mv_hi, start=False, stop=last)

            def free_acc(b, it=0, per=0):
                if b >= 2:
                    pe.wait_ge(acc_drained[b % 2], it * (per // 2) + b // 2)

            def norm_group(g, src):
                if g >= 4:
                    pe.wait_ge(norm_lo, g - 3)
                i = g % (KT // 2)
                for j in range(2):
                    for t in range(T):
                        mm = pe.transpose(aux[:, g % 4, S * j + P * t:S * j + P * (t + 1)],
                                          src[:, t, (2 * i + j) * P:(2 * i + j + 1) * P], ident[:, :])
                mm.then_inc(norm_turned, 1)

            def turn_natural(src, sem_turned):
                for i in range(4):
                    for t in range(T):
                        mm = pe.transpose(turn[i // 2][:, (i % 2) * S + t * P:(i % 2) * S + (t + 1) * P],
                                          src[:, t, i * P:(i + 1) * P], ident[:, :])
                mm.then_inc(sem_turned, 1)

            def stored(n):
                if not (isinstance(n, int) and n == 0):
                    pe.wait_ge(block_a, n)
                    pe.wait_ge(block_b, n)

            def turn_gated(g, i, mixed):
                pe.wait_ge(gated_ready, g + 1)
                if not (isinstance(mixed, int) and mixed == 0):
                    pe.wait_ge(mix_lo, mixed)
                turn_natural(gated[i], gated_turned)

            pe.wait_ge(ident_in, 16)
            for _ in range(WARM_UP):
                pe.transpose(turn[1][:, 0:P], ident[:, :], ident[:, :])
            for g in range(AHEAD):
                pe.wait_ge(mem_in[g * 2 * P // PIECE], 16)
                norm_group(g, nat)
                if g == 0:
                    pe.wait_ge(gains_in, 16 * 3)
                    pe.transpose(aux[:, 3, 0:GAINS], gain_rows, ident[0:GAINS, 0:GAINS]).then_inc(gains_turned, 1)
            pe.wait_ge(gains_ready, 1)

            def kv(layer):
                c0, b0 = SECTIONS[f"KV{layer}"]
                src = (b_hi, b_lo) if layer == 0 else (a_hi, a_lo)
                for s in range(4 * BLK):
                    b, i = divmod(s, BLK)
                    if i == 0:
                        free_acc(b0 + b)
                    if s < KT // 2:
                        if layer == 0:
                            pe.wait_ge(norm_lo, s + 1)
                        else:
                            pe.wait_ge(tile_lo, 8)
                    chunk(c0 + s, s % RING, (b0 + b) % 2, i, BLK, *src)
                    if layer == 0 and s + AHEAD < KT // 2:
                        pe.wait_ge(mem_in[(s + AHEAD) * 2 * P // PIECE], 16)
                        norm_group(s + AHEAD, nat)
                    if 20 <= s < 20 + KT // 2:
                        if layer == 0:
                            pe.wait_ge(x_in, 16 * (D // PIECE))
                        else:
                            pe.wait_ge(h_ready, 2)
                        stored(B_KV[layer] + 2)
                        norm_group((layer + 1) * KT // 2 + s - 20, h)
                    for p in range(2):
                        if s == BLK * (p + 1) + 1:
                            n = B_KV[layer] + p
                            drained(pe, b0 + p)
                            stored(n)
                            if layer == 0:
                                pe.wait_ge(norm_lo, KT // 2)
                            turn_natural(block, block_turned)

            def memory(layer):
                c0, b0 = SECTIONS[f"MEM{layer}"]
                for s in range(4 * BLK):
                    b, i = divmod(s, BLK)
                    if i == 0:
                        free_acc(b0 + b)
                    if s < KT // 2:
                        pe.wait_ge(norm_lo, (2 * layer + 1) * KT // 2 + s + 1)
                    chunk(c0 + s, s % RING, (b0 + b) % 2, i, BLK, a_hi, a_lo)
                    if layer == 1 and s == 3:
                        pe.wait_ge(roped, ROPE_SHARED + 1)
                        turn_natural(block, block_turned)
                    for p in range(2):
                        n, u, x = B_MEM[layer] + p, U_MEM[layer] + p, X_MEM[layer] + p
                        if s == 9 + BLK * p:
                            drained(pe, b0 + p)
                            stored(n)
                            if x:
                                pe.wait_ge(probs_a, x)
                                pe.wait_ge(probs_b, x)
                            turn_natural(block, block_turned)
                        if s == 11 + BLK * p:
                            stored(n + 1)
                            if u:
                                pe.wait_ge(o_stored, u)
                            for t in range(T):
                                for j in range(2):
                                    for d in range(2):
                                        k, tok = 2 * j + d, slice(t * P, (t + 1) * P)
                                        mm = three_passes(score[t][:, S * j:S * (j + 1)], mem_q_hi[:, k, tok],
                                                          mem_q_lo[:, k, tok], mem_kt[:, 4 * p + k, :],
                                                          mem_kt_lo[:, 4 * p + k, :], d == 0, d == 1)
                            mm.then_inc(score_full, 1)
                        if s == 14 + BLK * p:
                            pe.wait_ge(probs_ready, x + 1)
                            for j in range(2):
                                for m in range(2):
                                    for t in range(T):
                                        mm = pe.transpose(turn[j][:, m * S + t * P:m * S + (t + 1) * P],
                                                          mem_p[:, t, j, m * P:(m + 1) * P], ident[:, :])
                            mm.then_inc(probs_turned, 1)
                        if s == 16 + BLK * p:
                            pe.wait_ge(probs_a, x + 1)
                            pe.wait_ge(probs_b, x + 1)
                            drained(pe, SECTIONS[f"KV{layer}"][1] + 2 + p)
                            for t in range(T):
                                for j in range(2):
                                    for m in range(2):
                                        k, tok = 2 * j + m, slice(t * P, (t + 1) * P)
                                        cols = slice((2 * p + j) * RET_DIM, (2 * p + j + 1) * RET_DIM)
                                        mm = three_passes(score[t][:, RET_DIM * j:RET_DIM * (j + 1)],
                                                          mem_pt_hi[:, k, tok], mem_pt_lo[:, k, tok],
                                                          mem_v[:, m, cols], mem_v_lo[:, m, cols], m == 0, m == 1)
                            mm.then_inc(o_full, 1)
                    if s == 26:
                        turn_gated(GROUPS * layer, 0, GROUPS * layer)

            kv(0)
            memory(0)

            c0, b0 = SECTIONS["RET"]
            with pe.Fori(0, 4) as it:
                for s in range(4 * BLK):
                    b, i = divmod(s, BLK)
                    if i == 0:
                        free_acc(b0 + b, it, 4)
                    chunk(it * (4 * BLK) + (c0 + s), s % RING, (b0 + b) % 2, i, BLK, a_hi, a_lo)
                    if s == 2:
                        turn_gated(it + 1, 1, it + 1)
                    for j in range(2):
                        if s == 11 + BLK * j:
                            pe.wait_ge(roped, it * 2 + (ROPE_RET + j + 1))
                            stored(it * 2 + (B_RET + j))
                            if j == 0:
                                pe.wait_ge(mix_lo, it + 2)
                            turn_natural(block, block_turned)
                    if s == 22:
                        stored(it * 2 + (B_RET + 2))
                        pe.wait_ge(o_stored, it + U_RET)
                        for j in range(2):
                            for q0, q1, k0, c in ((0, S, 0, 0), (P, S, P, S)):
                                for d in range(2):
                                    k = 2 * j + d
                                    mm = three_passes(score[j][:, c:c + q1 - q0], ret_k_hi[:, k, k0:k0 + P],
                                                      ret_k_lo[:, k, k0:k0 + P], ret_q_hi[:, k, q0:q1],
                                                      ret_q_lo[:, k, q0:q1], d == 0, d == 1)
                        mm.then_inc(score_full, 1)
                    if s == 25:
                        pe.wait_ge(masked_ready, it + 1)
                        drained(pe, b0 + 2, it, 4)
                        for t in range(T):
                            for j in range(2):
                                cols = slice(RET_DIM * j, RET_DIM * (j + 1))
                                for m in range(t + 1):
                                    at = m * S + (t - m) * P
                                    mm = pe.matmul(score[t][:, cols], masked[:, j, at:at + P], v_nat[:, m, cols],
                                                   start=(m == 0), stop=(m == t))
                        mm.then_inc(o_full, 1)

            def out_pass(layer, it):
                c0, b0 = SECTIONS[f"OUT{layer}"]
                for b in range(2):
                    for i in range(OBLK):
                        s = OBLK * b + i
                        if i == 0:
                            free_acc(b0 + b, it, 2)
                        if it == 0 and s == 7:
                            pe.wait_ge(mix_lo, GROUPS * (layer + 1))
                        chunk(it * (2 * OBLK) + (c0 + s), s % RING, (b0 + b) % 2, i, OBLK, b_hi, b_lo)
                        if it == 0 and s == 2:
                            turn_gated(GROUPS * (layer + 1) - 1, 1, GROUPS * (layer + 1) - 1)
                        if layer == 0 and s in (7, 10, 13, 16):
                            g = (s - 7) // 3
                            pe.wait_ge(mem_tile_in, it * 16 + 16)
                            for j in range(4):
                                mm = pe.transpose(aux[:, g, P * j:P * (j + 1)],
                                                  mem_tile[:, (4 * g + j) * P:(4 * g + j + 1) * P], ident[:, :])
                            mm.then_inc(tile_turned, 1)

            pe.wait_ge(mix_lo, GROUPS - 1)
            pe.wait_ge(o_stored, U_MEM[1])
            for it in range(2):
                out_pass(0, it)
            kv(1)
            c0, b0 = SECTIONS["SHARED"]
            for s in range(BLK):
                if s == 0:
                    free_acc(b0)
                pe.wait_ge(norm_lo, KT + s + 1)
                chunk(c0 + s, s % RING, b0 % 2, s, BLK, b_hi, b_lo)
                norm_group(3 * KT // 2 + s, h)
            memory(1)

            c0, b0 = SECTIONS["SWA"]
            with pe.Fori(0, 2) as it:
                for s in range(4 * BLK):
                    b, i = divmod(s, BLK)
                    if i == 0:
                        free_acc(b0 + b, it, 4)
                    chunk(it * (4 * BLK) + (c0 + s), s % RING, (b0 + b) % 2, i, BLK, a_hi, a_lo)
                    if s == 2:
                        turn_gated(it * 2 + (GROUPS + 1), 1, it * 2 + (GROUPS + 1))
                    for p, u in units_at(s, 5):
                        x = it * (2 * UNITS) + (X_SWA + UNITS * p + u)
                        un = it * (2 * UNITS) + (U_SWA + UNITS * p + u)
                        pe.wait_ge(probs_a, x + 1)
                        pe.wait_ge(probs_b, x + 1)
                        pe.wait_ge(o_stored, un)
                        if UNITS * p + u + 2 < 2 * UNITS:
                            pe.wait_ge(neg_ready, x + 3)
                        for e in range(2):
                            for t in range(T):
                                for m in range(t + 1):
                                    at = (t + m) * P
                                    mm = pe.matmul(score[e][:, 3 * P + SWA_DIM * t:3 * P + SWA_DIM * (t + 1)],
                                                   swa_pt[:, u % 2, e, at:at + P],
                                                   swa_v[:, m, p * SWA_DIM:(p + 1) * SWA_DIM],
                                                   start=(m == 0), stop=(m == t))
                        mm.then_inc(o_full, 1)
                    for p, u in units_at(s, 0):
                        x = it * (2 * UNITS) + (X_SWA + UNITS * p + u)
                        if u == 0:
                            stored(it * 2 + (B_SWA + p + 1))
                            pe.wait_ge(copies_ready, it + 1)
                        if (p, u) == (0, 0):
                            pe.wait_ge(o_stored, it * (2 * UNITS) + U_SWA)
                        pe.wait_ge(neg_ready, x)
                        pe.wait_ge(o_stored, it * (2 * UNITS) + (U_SWA + UNITS * p + u - 2))
                        for e in range(2):
                            half = slice(64 * e, 64 * e + 64)
                            pe.matmul(score[e][:, 0:P], q_t[half, u, 0:P], swa_kt[half, p, 0:P], start=True, stop=True)
                            mm = pe.matmul(score[e][:, P:3 * P], q_t[half, u, P:S], swa_kt[half, p, :], start=True, stop=True)
                        mm.then_inc(score_full, 1)
                    for p, u in units_at(s, 3):
                        x = it * (2 * UNITS) + (X_SWA + UNITS * p + u)
                        pe.wait_ge(probs_ready, x + 1)
                        pe.wait_ge(probs_a, x)
                        pe.wait_ge(probs_b, x)
                        if (p, u) == (0, 2):
                            stored(it * 2 + (B_SWA + 2))
                        if (p, u) == (1, 3):
                            pe.wait_ge(mix_lo, it * 2 + (GROUPS + 3))
                        for e in range(2):
                            for j in range(3):
                                mm = pe.transpose(turn[e][:, P * j:P * (j + 1)], swa_p[:, u % 2, e, P * j:P * (j + 1)], ident[:, :])
                        mm.then_inc(probs_turned, 1)
                    for p in range(2):
                        if s == 9 + BLK * p:
                            pe.wait_ge(roped, it * 2 + (ROPE_SWA + p + 1))
                            if p == 0:
                                pe.wait_ge(mix_lo, it * 2 + (GROUPS + 2))
                            pe.wait_ge(probs_a, it * (2 * UNITS) + (X_SWA + 2 * p))
                            pe.wait_ge(probs_b, it * (2 * UNITS) + (X_SWA + 2 * p))
                            turn_natural(block, block_turned)
                    if s == 27:
                        pe.wait_ge(probs_a, it * (2 * UNITS) + (X_SWA + 7))
                        pe.wait_ge(probs_b, it * (2 * UNITS) + (X_SWA + 7))
                        turn_gated(it * 2 + (GROUPS + 2), 0, it * 2 + (GROUPS + 2))
            pe.wait_ge(mix_lo, 2 * GROUPS - 1)
            for it in range(2):
                out_pass(1, it)


def _constants():
    import numpy as np
    ident = np.eye(P, dtype=np.float32)
    ret = np.float32(10000.0) ** (-np.arange(0, RET_DIM, 2, dtype=np.float32) / np.float32(RET_DIM))
    swa = np.float32(500000.0) ** (-np.arange(0, ROT, 2, dtype=np.float32) / np.float32(ROT))
    freq = np.broadcast_to(np.concatenate([ret, swa]).astype(np.float32), (P, FREQS)).copy()
    m, q = np.arange(P)[:, None], np.arange(S)[None, :]
    gamma = np.log1p(-np.exp2(-5.0 - np.arange(RET_HEADS)))
    full = np.where(q >= m, np.exp(gamma[:, None, None] * np.maximum(q - m, 0)), 0.0) * RET_DIM ** -0.5
    decay = np.concatenate([full, full[:, :, 0:P]], axis=2).transpose(1, 0, 2).astype(np.float32).copy()
    q, k = np.arange(P)[:, None], np.arange(P)[None, :]
    own, before = np.where(k <= q, 0.0, -1e30), np.where(k > q, 0.0, -1e30)
    band = np.concatenate([own, before, own], axis=1).astype(np.float32)
    return {"c_ident": ident, "c_freq": freq, "c_decay": decay, "c_band": band}


_INS = ["x", "mem", "positions", "pre_norm_g", "post_norm_g", "mem_norm_g", "kv_norm_g",
        "w_in_a", "w_in_b", "w_kv_b", "sinks_b", "w_mem_kv", "w_out"]


def kernel(**inputs):
    import numpy as np
    from concourse import bacc
    from concourse.bass_utils import run_bass_kernel_spmd

    nc = bacc.Bacc("TRN2", target_bir_lowering=False, num_devices=1)
    arrays = {f"in_{name}": np.ascontiguousarray(inputs[name]) for name in _INS}
    arrays.update(_constants())
    args = [nc.dram_tensor(name, a.shape, mybir.dt.from_np(a.dtype), kind="ExternalInput").ap()
            for name, a in arrays.items()]
    out = nc.dram_tensor("out_h", (1, S, D), F32, kind="ExternalOutput").ap()
    trunk(nc, *args, out)
    result = run_bass_kernel_spmd(nc, [arrays], core_ids=[0])
    return result.results[0]["out_h"]
```
